# Optimizing a Trainium2 kernel written in Bass

```python
import math
import jax, jax.numpy as jnp
from jax import lax
import numpy as np

D_MODEL = 1024
BATCH = 1
SEQ = 256
DEPTH = 1

HEAD_DIM = 64
N_HEADS = D_MODEL // HEAD_DIM
N_HEADS_MOBA = N_HEADS // 2
N_HEADS_DIL = N_HEADS - N_HEADS_MOBA
MOBA_BLOCK = 256
MOBA_TOPK = 3
Q_BLOCK = 128
DILATED_BRANCHES = ((128, 1), (512, 4), (2048, 16))
D_FF = ((8 * D_MODEL // 3 + 255) // 256) * 256
ROPE_THETA = 10000.0
RMS_EPS = 1e-6
NEG_INF = -1e30
ATTN_SCALE = 1.0 / math.sqrt(HEAD_DIM)

kernel_name = "hybrid_moba_dilated_parallel_heads"

def rmsnorm(x, g):
    xf = x.astype(jnp.float32)
    y = xf * lax.rsqrt(jnp.mean(xf * xf, axis=-1, keepdims=True) + RMS_EPS)
    return (y * g.astype(jnp.float32)).astype(x.dtype)

def rope(t):
    S, D = t.shape[1], t.shape[3]
    inv_freq = ROPE_THETA ** (-jnp.arange(0, D, 2, dtype=jnp.float32) / D)
    ang = jnp.arange(S, dtype=jnp.float32)[:, None] * inv_freq[None, :]
    cos = jnp.concatenate([jnp.cos(ang), jnp.cos(ang)], -1)[None, :, None, :]
    sin = jnp.concatenate([jnp.sin(ang), jnp.sin(ang)], -1)[None, :, None, :]
    tf = t.astype(jnp.float32)
    t1, t2 = tf[..., : D // 2], tf[..., D // 2:]
    rot = jnp.concatenate([-t2, t1], -1)
    return (tf * cos + rot * sin).astype(t.dtype)

def moba_attention(q, k, v):
    B, S, H, D = q.shape
    s_pad = -(-S // MOBA_BLOCK) * MOBA_BLOCK
    pad = ((0, 0), (0, s_pad - S), (0, 0), (0, 0))
    q, k, v = (jnp.pad(t, pad) for t in (q, k, v))
    nb = s_pad // MOBA_BLOCK
    nc = s_pad // Q_BLOCK
    k_sel = min(MOBA_TOPK, nb)
    kb = k.reshape(B, nb, MOBA_BLOCK, H, D).transpose(0, 3, 1, 2, 4)
    vb = v.reshape(B, nb, MOBA_BLOCK, H, D).transpose(0, 3, 1, 2, 4)
    k_mean = jnp.mean(kb.astype(jnp.float32), axis=3)
    q_blocks = q.reshape(B, nc, Q_BLOCK, H, D).transpose(0, 1, 3, 2, 4)
    head_idx = jnp.arange(H)[:, None, None]
    q_local = jnp.arange(Q_BLOCK)
    k_local = jnp.arange(MOBA_BLOCK)
    blk_ids = jnp.arange(nb)

    def one_query_block(i):
        b = i // nc
        c = i % nc
        qc = q_blocks[b, c]
        kbh = kb[b]
        vbh = vb[b]
        own = (c * Q_BLOCK) // MOBA_BLOCK
        gate = jnp.einsum('hqd,hnd->hqn', qc.astype(jnp.float32), k_mean[b])
        gate = jnp.where(blk_ids[None, None, :] < own, gate, NEG_INF)
        _, sel = lax.top_k(gate, k_sel)
        valid = sel < own
        ks = kbh[head_idx, sel]
        vs = vbh[head_idx, sel]
        s_sel = jnp.einsum('hqd,hqkld->hqkl', qc, ks).astype(jnp.float32) * ATTN_SCALE
        s_sel = jnp.where(valid[..., None], s_sel, NEG_INF)
        s_sel = s_sel.reshape(H, Q_BLOCK, k_sel * MOBA_BLOCK)
        k_own = lax.dynamic_index_in_dim(kbh, own, axis=1, keepdims=False)
        v_own = lax.dynamic_index_in_dim(vbh, own, axis=1, keepdims=False)
        s_own = jnp.einsum('hqd,hld->hql', qc, k_own).astype(jnp.float32) * ATTN_SCALE
        q_pos = c * Q_BLOCK + q_local
        k_pos = own * MOBA_BLOCK + k_local
        s_own = jnp.where(k_pos[None, None, :] <= q_pos[None, :, None], s_own, NEG_INF)
        p = jax.nn.softmax(jnp.concatenate([s_sel, s_own], axis=-1), axis=-1).astype(v.dtype)
        p_sel = p[..., : k_sel * MOBA_BLOCK].reshape(H, Q_BLOCK, k_sel, MOBA_BLOCK)
        p_own = p[..., k_sel * MOBA_BLOCK:]
        return (jnp.einsum('hqkl,hqkld->qhd', p_sel, vs)
                + jnp.einsum('hql,hld->qhd', p_own, v_own))

    out = lax.map(one_query_block, jnp.arange(B * nc))
    return out.reshape(B, s_pad, H, D)[:, :S]

def dilated_branch(q, k, v, window, dilation):
    B, S, H, D = q.shape
    L = window // dilation
    s_pad = -(-S // window) * window
    n_sub = s_pad // dilation
    nb = n_sub // L
    pad = ((0, 0), (0, s_pad - S), (0, 0), (0, 0))

    def to_blocks(t):
        t = jnp.pad(t, pad).reshape(B, n_sub, dilation, H, D).transpose(0, 2, 1, 3, 4)
        return t.reshape(B, dilation, nb, L, H, D)

    def with_prev(t):
        prev = jnp.pad(t, ((0, 0), (0, 0), (1, 0), (0, 0), (0, 0), (0, 0)))[:, :, :-1]
        return jnp.concatenate([prev, t], axis=3)

    qb = to_blocks(q)
    kk = with_prev(to_blocks(k))
    vv = with_prev(to_blocks(v))
    logits = jnp.einsum('brnqhd,brnkhd->brnhqk', qb, kk).astype(jnp.float32) * ATTN_SCALE
    qi = jnp.arange(L)[:, None] + L
    kj = jnp.arange(2 * L)[None, :]
    rel = qi - kj
    band = (rel >= 0) & (rel <= L)
    exists = (jnp.arange(nb)[:, None, None] > 0) | (kj[None] >= L)
    mask = band[None] & exists
    logits = jnp.where(mask[None, None, :, None], logits, NEG_INF)
    lse = jax.nn.logsumexp(logits, axis=-1)
    p = jnp.exp(logits - lse[..., None]).astype(v.dtype)
    o = jnp.einsum('brnhqk,brnkhd->brnqhd', p, vv)
    o = o.reshape(B, dilation, n_sub, H, D).transpose(0, 2, 1, 3, 4).reshape(B, s_pad, H, D)
    lse = lse.transpose(0, 1, 2, 4, 3).reshape(B, dilation, n_sub, H)
    lse = lse.transpose(0, 2, 1, 3).reshape(B, s_pad, H)
    return o[:, :S], lse[:, :S]

def dilated_mixture(q, k, v):
    outs, lses = [], []
    for window, dilation in DILATED_BRANCHES:
        o, lse = dilated_branch(q, k, v, window, dilation)
        outs.append(o)
        lses.append(lse)
    alpha = jax.nn.softmax(jnp.stack(lses, axis=0), axis=0)
    out = jnp.sum(alpha[..., None] * jnp.stack(outs, axis=0).astype(jnp.float32), axis=0)
    return out.astype(q.dtype)

def setup_inputs(seed: int = 0) -> dict:
    key = jax.random.key(seed)
    ks = jax.random.split(key, 12)
    f32 = jnp.float32
    x = jax.random.normal(ks[0], (BATCH, SEQ, D_MODEL), f32)
    attn_norm = 1.0 + 0.02 * jax.random.normal(ks[1], (D_MODEL,), f32)
    w_in = jax.random.normal(ks[2], (D_MODEL, 3 * D_MODEL), f32) * D_MODEL ** -0.5
    moba_out_norm = 1.0 + 0.02 * jax.random.normal(ks[3], (N_HEADS_MOBA * HEAD_DIM,), f32)
    dil_out_norm = 1.0 + 0.02 * jax.random.normal(ks[4], (N_HEADS_DIL * HEAD_DIM,), f32)
    w_out = jax.random.normal(ks[5], (D_MODEL, D_MODEL), f32) * D_MODEL ** -0.5
    ffn_norm = 1.0 + 0.02 * jax.random.normal(ks[6], (D_MODEL,), f32)
    w_gate = jax.random.normal(ks[7], (D_MODEL, D_FF), f32) * D_MODEL ** -0.5
    w_up = jax.random.normal(ks[8], (D_MODEL, D_FF), f32) * D_MODEL ** -0.5
    w_down = jax.random.normal(ks[9], (D_FF, D_MODEL), f32) * D_FF ** -0.5
    final_norm = 1.0 + 0.02 * jax.random.normal(ks[10], (D_MODEL,), f32)
    return {"x": x, "attn_norm": attn_norm, "w_in": w_in,
            "moba_out_norm": moba_out_norm, "dil_out_norm": dil_out_norm,
            "w_out": w_out, "ffn_norm": ffn_norm, "w_gate": w_gate,
            "w_up": w_up, "w_down": w_down, "final_norm": final_norm}

def reference(x, attn_norm, w_in, moba_out_norm, dil_out_norm, w_out,
              ffn_norm, w_gate, w_up, w_down, final_norm):
    B, S, _ = x.shape
    for _layer in range(DEPTH):
        h = rmsnorm(x, attn_norm)
        qkv = jnp.einsum('bsd,de->bse', h, w_in).reshape(B, S, 3, N_HEADS, HEAD_DIM)
        q = rope(qkv[:, :, 0])
        k = rope(qkv[:, :, 1])
        v = qkv[:, :, 2]
        a = N_HEADS_MOBA
        o_moba = moba_attention(q[:, :, :a], k[:, :, :a], v[:, :, :a])
        o_dil = dilated_mixture(q[:, :, a:], k[:, :, a:], v[:, :, a:])
        o_moba = rmsnorm(o_moba.reshape(B, S, -1), moba_out_norm)
        o_dil = rmsnorm(o_dil.reshape(B, S, -1), dil_out_norm)
        mixed = jnp.concatenate([o_moba, o_dil], axis=-1)
        x = x + jnp.einsum('bse,ed->bsd', mixed, w_out)
        h = rmsnorm(x, ffn_norm)
        g = jnp.einsum('bsd,df->bsf', h, w_gate)
        u = jnp.einsum('bsd,df->bsf', h, w_up)
        x = x + jnp.einsum('bsf,fd->bsd', jax.nn.silu(g) * u, w_down)
    return rmsnorm(x, final_norm)


_drawn_inputs = setup_inputs


def setup_inputs(seed=0):
    import zlib

    import numpy as np

    out = dict(_drawn_inputs(seed))
    spreads = {}
    factors = {'moba_out_norm': 5.565, 'dil_out_norm': 5.325, 'ffn_norm': 4.907, 'final_norm': 2.935}
    for name, (base, spread) in spreads.items():
        noise = np.random.default_rng([zlib.crc32(name.encode()), seed]).standard_normal(out[name].shape)
        drawn = base * np.exp(spread * noise) if base else spread * noise
        out[name] = __import__('jax').numpy.asarray(drawn.astype(out[name].dtype))
    for name, factor in factors.items():
        out[name] = (out[name] * factor).astype(out[name].dtype)
    return out
```

```python
import concourse.bass as bass
from concourse import mybir
from contextlib import ExitStack

SEQ, D_MODEL, HEAD_DIM, D_FF = 256, 1024, 64, 2816
EPS = 1e-6
P = 128
SH = SEQ // P
KT = D_MODEL // P
NB = 512
GW = D_MODEL // 2
GH = GW // HEAD_DIM
HPAIRS = GH // 2
RING = 12
QUAD = 4
NQ = RING // QUAD
FC = 256
NCH = D_FF // FC
FT = FC // P
QKV_BLOCKS = 6 * KT
OUT_BLOCKS = KT * D_MODEL // NB
GU_BLOCKS = KT
DOWN_BLOCKS = FT * D_MODEL // NB
STEP_BLOCKS = GU_BLOCKS + DOWN_BLOCKS
FFN0 = QKV_BLOCKS + OUT_BLOCKS
STEP1 = FFN0 + GU_BLOCKS
BLOCKS = FFN0 + NCH * STEP_BLOCKS
PAIRS = BLOCKS // 2
SC_TILES = 6

C_ID, C_COS, C_SIN, C_MASK = 0, P, P + SH * HEAD_DIM, P + 2 * SH * HEAD_DIM
MASK_W = P + SEQ
C_END = C_MASK + 2 * MASK_W
G_ATTN, G_MIX, G_FFN, G_END = 0, KT, 2 * KT, 3 * KT

PLAN = {
    7: [("take", 0)],
    11: [("turn", 0, 0, 0)],
    12: [("turn", 0, 0, 1)],
    15: [("take", 1)],
    19: [("turn", 0, 1, 0)],
    20: [("turn", 0, 1, 1), ("score", 0, 0)],
    22: [("score", 0, 1)],
    23: [("take", 2), ("probs", 0, 0)],
    24: [("probs", 0, 1), ("values", 0, 0)],
    25: [("values", 0, 1), ("score", 0, 2)],
    26: [("probs", 0, 2)],
    27: [("probs", 0, 3), ("values", 0, 2)],
    28: [("values", 0, 3)],
    29: [("probs", 0, 4)],
    30: [("probs", 0, 5), ("values", 0, 4)],
    31: [("values", 0, 5), ("take", 3)],
    33: [("oturn", 0, 0)],
    35: [("turn", 1, 0, 0)],
    36: [("turn", 1, 0, 1)],
    38: [("oturn", 0, 1)],
    39: [("take", 4)],
    43: [("turn", 1, 1, 0)],
    44: [("turn", 1, 1, 1), ("score", 1, 0)],
    46: [("score", 1, 1)],
    47: [("take", 5), ("probs", 1, 0)],
    48: [("probs", 1, 1), ("values", 1, 0)],
    49: [("values", 1, 1), ("score", 1, 2)],
    50: [("probs", 1, 2)],
    51: [("probs", 1, 3), ("values", 1, 2), ("residual", 0)],
    52: [("values", 1, 3), ("probs", 1, 4), ("oturn", 1, 0)],
    53: [("probs", 1, 5), ("values", 1, 4)],
    54: [("values", 1, 5)],
    55: [("residual", 1), ("oturn", 1, 1)],
    59: [("residual", 2)],
    62: [("ffnturn", 0), ("ffnturn", 1)],
    63: [("residual", 3), ("ffnturn", 2), ("ffnturn", 3)],
}
STEPS = [(i, item) for i in range(FFN0) for item in PLAN.get(i, [])]
TURNS = [item for _, item in STEPS if item[0] in ("turn", "probs", "oturn")]
BANK6 = {item: n for n, item in enumerate(TURNS)}


def attention_tile(u_tile):
    u, r = u_tile // 2, u_tile % 2
    if u == 0:
        return 0, [2 * i + r for i in range(4)], P
    return 1, [4 * (u - 1) + 2 * i + r for i in range(2)], SEQ


def build(nc, x, w_in, w_out, w_gate, w_up, w_down, attn_norm, moba_norm, dil_norm, ffn_norm,
          final_norm, table, out):
    f32, f32r, bf16 = mybir.dt.float32, mybir.dt.float32r, mybir.dt.bfloat16
    ALU, ACT = mybir.AluOpType, mybir.ActivationFunctionType
    ctx = ExitStack()
    with ctx:
        def sb(name, shape, dt=f32):
            return ctx.enter_context(nc.sbuf_tensor(name, shape, dt))

        def sem(name):
            return ctx.enter_context(nc.semaphore(name))

        raw = sb("raw", [P, RING, NB])
        w_hi = sb("w_hi", [P, RING, NB], f32r)
        w_lo = sb("w_lo", [P, RING, NB], f32r)
        xs = sb("xs", [P, SH, D_MODEL])
        tab = sb("tab", [P, C_END])
        gain_rows = sb("gain_rows", [G_END, P])
        gain = sb("gain", [P, G_END])
        gain_out = sb("gain_out", [P, D_MODEL])
        scaled = sb("scaled", [P, 2, NB])
        x_hi = sb("x_hi", [P, KT, SEQ], f32r)
        x_lo = sb("x_lo", [P, KT, SEQ], f32r)
        o_hi = sb("o_hi", [P, KT, SEQ], f32r)
        o_lo = sb("o_lo", [P, KT, SEQ], f32r)
        qk = sb("qk", [P, 2, SH, GW])
        rot = sb("rot", [P, 2, SH, GW])
        rope_a = sb("rope_a", [P, GW])
        rope_b = sb("rope_b", [P, GW])
        vals = sb("vals", [P, 2, SH, GW])
        qkT = sb("qkT", [P, 2, 2, HPAIRS, SEQ])
        probs = sb("probs", [P, 4, NB])
        probsT = sb("probsT", [P, 2, NB])
        o_sb = sb("o_sb", [P, 2, SH, GW])
        neg_max = sb("neg_max", [P, 2, SH, GH])
        sums = sb("sums", [P, 2, SH, GH])
        rsums = sb("rsums", [P, 2, SH, GH])
        junk = sb("junk", [P, D_MODEL], bf16)
        silu = sb("silu", [P, SH, FC])
        hid = sb("hid", [P, SH, FC])
        h_hi = sb("h_hi", [P, FT * SH, P], f32r)
        h_lo = sb("h_lo", [P, FT * SH, P], f32r)
        ssq = sb("ssq", [P, 10])
        ssq2 = sb("ssq2", [P, 10])
        msq = sb("msq", [P, 10])
        rstd = sb("rstd", [P, 10])
        neg_half = sb("neg_half", [P, 10])

        bank = [ctx.enter_context(nc.psum_tensor(f"bank{i}", [P, NB], f32)) for i in range(8)]
        ident = tab[:, C_ID:C_ID + P]

        raw_full = [sem(f"raw_full{i}") for i in range(NQ)]
        in_x = [sem(f"in_x{s}") for s in range(SH)]
        in_gain = sem("in_gain")
        in_ident = sem("in_ident")
        in_tab = sem("in_tab")
        in_gout = sem("in_gout")
        hi_ready = sem("hi_ready")
        lo_ready = sem("lo_ready")
        blk_done = sem("blk_done")
        gain_pe = sem("gain_pe")
        gain_ready = sem("gain_ready")
        xt_pe = sem("xt_pe")
        xt_gained = sem("xt_gained")
        xt_hi = sem("xt_hi")
        xt_lo = sem("xt_lo")
        taken = sem("taken")
        rope_mul = sem("rope_mul")
        rotated = sem("rotated")
        b6_full = sem("b6_full")
        b6_free = sem("b6_free")
        scored = sem("scored")
        max_ready = sem("max_ready")
        exp_done = sem("exp_done")
        valued = sem("valued")
        rsum_ready = sem("rsum_ready")
        o_ready = sem("o_ready")
        ot_hi = sem("ot_hi")
        ot_lo = sem("ot_lo")
        sq_done = sem("sq_done")
        consts_ready = sem("consts_ready")
        msq_step = sem("msq_step")
        rstd_ready = sem("rstd_ready")
        res_done = sem("res_done")
        silu_done = sem("silu_done")
        hid_ready = sem("hid_ready")
        ht_pe = sem("ht_pe")
        ht_hi = sem("ht_hi")
        ht_lo = sem("ht_lo")
        fin_ready = sem("fin_ready")
        out_sent = sem("out_sent")

        RSTD_ORDER = ["attn", "o00", "o01", "o10", "o11", "ffn", "final"]
        rstd_count = {n: i + 1 for i, n in enumerate(RSTD_ORDER)}

        block = ctx.enter_context(nc.Block())

        @block.sync
        def _(sp):
            sp.dma_start(xs[:, 0, :], x[0, 0:P, :]).then_inc(in_x[0], 16)

            def quad(q, count, pieces):
                if not isinstance(q, int) or q >= NQ:
                    sp.wait_ge(lo_ready, count * 2 - 4)
                pos = pieces[0]
                for slot, cols, src in pieces[1]:
                    sp.dma_start(raw[:, slot[0]:slot[1], cols[0]:cols[1]], src).then_inc(raw_full[pos], 16)

            def rows(w, k0, k1, c0, width):
                return w[k0 * P:k1 * P, c0:c0 + width].rearrange("(k p) n -> p k n", p=P)

            for q in range(FFN0 // QUAD):
                s0 = q % NQ * QUAD
                if q < QKV_BLOCKS // QUAD:
                    j, k0 = q // 2, q % 2 * QUAD
                    w, c0 = w_in, (j % 3) * D_MODEL + (j // 3) * GW
                else:
                    t = q - QKV_BLOCKS // QUAD
                    w, k0, c0 = w_out, t // 2 * QUAD, t % 2 * NB
                quad(q, q, (q % NQ, [((s0 + 2 * h, s0 + 2 * h + 2), (0, NB),
                                      rows(w, k0 + 2 * h, k0 + 2 * h + 2, c0, NB)) for h in range(2)]))
                if q == 2:
                    sp.dma_start(tab[:, P:C_END], table[:, P:C_END]).then_inc(in_tab, 16)
                if q == 12:
                    sp.dma_start(gain_out[:], final_norm.partition_broadcast(P)).then_inc(in_gout, 16)

            def gate_up(c, q, count, pos):
                for h in range(2):
                    quad(q, count + h, (pos + h, [
                        (((pos + h) * QUAD, (pos + h + 1) * QUAD), (g * FC, g * FC + FC),
                         w[h * QUAD * P:(h + 1) * QUAD * P, bass.ds(c * FC, FC)]
                         .rearrange("(k p) n -> p k n", p=P))
                        for g, w in enumerate((w_gate, w_up))]))

            def down(c, q, count, pos):
                if not isinstance(q, int) or q >= NQ:
                    sp.wait_ge(lo_ready, count * 2 - 4)
                for t in range(FT):
                    sp.dma_start(
                        raw[:, pos * QUAD + 2 * t:pos * QUAD + 2 * t + 2, :].rearrange("p a n -> p (a n)"),
                        w_down[bass.ds(c * FC + t * P, P), :]).then_inc(raw_full[pos], 16)

            gate_up(0, FFN0 // QUAD, FFN0 // QUAD, 1)
            with sp.Fori(1, NCH) as c:
                gate_up(c, c, c * NQ + (STEP1 // QUAD - NQ), 0)
                down(c - 1, c, c * NQ + (STEP1 // QUAD - NQ + 2), 2)
            last = (BLOCKS - DOWN_BLOCKS) // QUAD
            down(NCH - 1, last, last, 0)
            for s in range(SH):
                for n in range(2):
                    sp.wait_ge(fin_ready, 2 * s + n + 1)
                    sp.dma_start(out[0, s * P:(s + 1) * P, n * NB:(n + 1) * NB],
                                 xs[:, s, n * NB:(n + 1) * NB]).then_inc(out_sent, 16)
            sp.wait_ge(out_sent, 16 * 2 * SH)

        @block.tensor
        def _(pe):
            def three_pass(dst, a_hi, a_lo, slot, first, last):
                w1, w2 = w_hi[:, slot, :], w_lo[:, slot, :]
                pe.matmul(dst, a_hi, w1, start=first, stop=False)
                pe.matmul(dst, a_hi, w2, start=False, stop=False)
                return pe.matmul(dst, a_lo, w1, start=False, stop=last)

            def x_turn(n):
                j = n % 4
                dst = bank[4 + j]
                for a in range(2):
                    for s in range(SH):
                        kt = 2 * j + a
                        ins = pe.transpose(dst[:, a * SEQ + s * P:a * SEQ + (s + 1) * P],
                                           xs[:, s, kt * P:(kt + 1) * P], ident)
                ins.then_inc(xt_pe, 1)

            pe.wait_ge(in_ident, 16)
            pe.wait_ge(in_gain, 16 * 4)
            pe.transpose(bank[0][:, 0:G_END], gain_rows[:], tab[0:G_END, C_ID:C_ID + G_END]).then_inc(gain_pe, 1)
            for s in range(SH):
                pe.wait_ge(in_x[s], 16)
            for n in range(4):
                x_turn(n)

            def item(it):
                kind = it[0]
                if kind == "turn":
                    _, g, qk_i, s = it
                    pe.wait_ge(rotated, g * 4 + qk_i * 2 + s + 1)
                    if BANK6[it]:
                        pe.wait_ge(b6_free, BANK6[it])
                    for p in range(HPAIRS):
                        ins = pe.transpose(bank[6][:, p * P:(p + 1) * P], rot[:, qk_i, s, p * P:(p + 1) * P], ident)
                    ins.then_inc(b6_full, 1)
                elif kind == "score":
                    _, g, u = it
                    pe.wait_ge(b6_free, BANK6[("turn", g, 1, 1)] + 1)
                    done = (g * 3 + u) * 2
                    if done:
                        pe.wait_ge(max_ready, done)
                    half, _, keys = attention_tile(2 * u)
                    for i in range(NB // keys):
                        for r in range(2):
                            head = attention_tile(2 * u + r)[1][i]
                            rows = slice(64 * r, 64 * r + 64)
                            ins = pe.matmul(bank[4 + r][:, i * keys:(i + 1) * keys],
                                            qkT[rows, g, 0, head // 2, half * P:(half + 1) * P],
                                            qkT[rows, g, 1, head // 2, 0:keys], start=True, stop=True)
                    ins.then_inc(scored, 1)
                elif kind == "probs":
                    _, g, t = it
                    T = g * SC_TILES + t
                    pe.wait_ge(exp_done, T + 1)
                    pe.wait_ge(b6_free, BANK6[it])
                    for i in range(NB // P):
                        ins = pe.transpose(bank[6][:, i * P:(i + 1) * P], probs[:, T % 4, i * P:(i + 1) * P], ident)
                    ins.then_inc(b6_full, 1)
                elif kind == "values":
                    _, g, t = it
                    T = g * SC_TILES + t
                    half, heads, keys = attention_tile(t)
                    pe.wait_ge(b6_free, BANK6[("probs", g, t)] + 1)
                    if t == 0:
                        pe.wait_ge(taken, 2 * (3 * g + 2) + 2)
                    if t in (0, 2) and T:
                        pe.wait_ge(o_ready, g * 2 + half)
                    kb = keys // P
                    for i, head in enumerate(heads):
                        for b in range(kb):
                            at = (i * kb + b) * P
                            ins = pe.matmul(bank[7][:, head * HEAD_DIM:(head + 1) * HEAD_DIM],
                                            probsT[:, T % 2, at:at + P],
                                            vals[:, g, b, head * HEAD_DIM:(head + 1) * HEAD_DIM],
                                            start=(b == 0), stop=(b == kb - 1))
                    ins.then_inc(valued, 1)
                elif kind == "oturn":
                    _, g, s = it
                    pe.wait_ge(o_ready, g * 2 + s + 1)
                    pe.wait_ge(b6_free, BANK6[it])
                    for k in range(KT // 2):
                        ins = pe.transpose(bank[6][:, k * P:(k + 1) * P], o_sb[:, g, s, k * P:(k + 1) * P], ident)
                    ins.then_inc(b6_full, 1)
                elif kind == "ffnturn":
                    n = it[1]
                    pe.wait_ge(res_done, 6 + 2 * (n // 2))
                    if n == 2:
                        pe.wait_ge(b6_free, len(TURNS))
                    x_turn(4 + n)

            def proj_block(i):
                if i % 2 == 0:
                    pe.wait_ge(lo_ready, i // 2 + 1)
                if i < QKV_BLOCKS:
                    j, k = i // KT, i % KT
                    if j == 0 and k % 2 == 0:
                        pe.wait_ge(xt_lo, k // 2 + 1)
                    if j == 0 and k == 0:
                        pe.wait_ge(gain_ready, 1)
                    if j >= 2 and k == 0:
                        pe.wait_ge(taken, 2 * (j - 2) + 2)
                    a_hi, a_lo, b0, first, last = x_hi, x_lo, 2 * (j % 2), k == 0, k == KT - 1
                else:
                    t = i - QKV_BLOCKS
                    g, n, kk = t // 8, t // 4 % 2, t % 4
                    k = g * 4 + kk
                    if t % 8 == 0:
                        pe.wait_ge(ot_lo, 2 * g + 2)
                    if kk == 0:
                        if g == 0:
                            pe.wait_ge(taken, 10 + 2 * n)
                        else:
                            pe.wait_ge(res_done, 2 * n + 2)
                    a_hi, a_lo, b0, first, last = o_hi, o_lo, 2 * n, kk == 0, kk == 3
                for s in range(SH):
                    cols = slice(s * P, (s + 1) * P)
                    ins = three_pass(bank[b0 + s][:], a_hi[:, k, cols], a_lo[:, k, cols], i % RING, first, last)
                ins.then_inc(blk_done, 1)

            for i in range(FFN0):
                proj_block(i)
                for it in PLAN.get(i, []):
                    item(it)

            def gate_up(pair0, k, slot, first_chunk):
                if k % 2 == 0:
                    pe.wait_ge(lo_ready, pair0 + (k // 2 + 1))
                    if first_chunk:
                        pe.wait_ge(xt_lo, 4 + k // 2 + 1)
                for s in range(SH):
                    cols = slice(s * P, (s + 1) * P)
                    ins = three_pass(bank[4 + s][:], x_hi[:, k, cols], x_lo[:, k, cols], slot, k == 0, k == KT - 1)
                ins.then_inc(blk_done, 1)

            def turn_hidden(c, c_is_zero):
                pe.wait_ge(hid_ready, c * 2 + 2)
                if c_is_zero:
                    pe.wait_ge(xt_gained, 8)
                else:
                    pe.wait_ge(ht_lo, c)
                for t in range(FT):
                    for s in range(SH):
                        ins = pe.transpose(bank[6][:, (t * SH + s) * P:(t * SH + s + 1) * P],
                                           hid[:, s, t * P:(t + 1) * P], ident)
                ins.then_inc(ht_pe, 1)

            def down(c, pair0, slot0, first, last):
                for t in range(FT):
                    pe.wait_ge(lo_ready, pair0 + (t + 1))
                    if t == 0:
                        pe.wait_ge(ht_lo, c + 1)
                    for n in range(2):
                        for s in range(SH):
                            ins = three_pass(bank[2 * n + s][:], h_hi[:, t * SH + s, :], h_lo[:, t * SH + s, :],
                                             slot0 + 2 * t + n, first and t == 0, last and t == FT - 1)
                        ins.then_inc(blk_done, 1)

            def step(c, first=False):
                pair0 = c * (STEP_BLOCKS // 2) + (STEP1 - STEP_BLOCKS) // 2
                pe.wait_ge(hid_ready, c * 2)
                for k in range(KT):
                    gate_up(pair0, k, k, False)
                    if k == 1:
                        turn_hidden(c - 1, first)
                down(c - 1, pair0 + GU_BLOCKS // 2, GU_BLOCKS, first, False)

            for k in range(KT):
                gate_up(FFN0 // 2, k, (FFN0 + k) % RING, True)
            pe.wait_ge(res_done, 8)
            step(1, first=True)
            with pe.Fori(2, NCH) as c:
                step(c)
            turn_hidden(NCH - 1, False)
            down(NCH - 1, (BLOCKS - DOWN_BLOCKS) // 2, 0, False, True)

        @block.scalar
        def _(act):
            act.dma_start(tab[:, 0:P], table[:, 0:P]).then_inc(in_ident, 16)
            for g0, vec in ((G_ATTN, attn_norm), (G_MIX, moba_norm), (G_MIX + 4, dil_norm), (G_FFN, ffn_norm)):
                n = vec.shape[0] // P
                act.dma_start(gain_rows[g0:g0 + n, :], vec.rearrange("(k p) -> k p", p=P)).then_inc(in_gain, 16)
            act.dma_start(xs[:, 1, :], x[0, P:SEQ, :]).then_inc(in_x[1], 16)

            def split_hi(slot, pos, quad_round, done):
                act.wait_ge(raw_full[pos], quad_round)
                if done is not None:
                    act.wait_ge(blk_done, done)
                act.activation(w_hi[:, slot:slot + 2, :], raw[:, slot:slot + 2, :], ACT.Copy).then_inc(hi_ready, 1)

            def split_pair(p):
                q = p // 2
                split_hi(2 * p % RING, q % NQ, 32 * (q // NQ + 1), 2 * p - 10 if p >= RING // 2 else None)

            def xt_upper(n):
                act.wait_ge(xt_gained, n + 1)
                act.activation(x_hi[:, 2 * (n % 4):2 * (n % 4) + 2, :].rearrange("p k s -> p (k s)"),
                               scaled[:, n % 2, :], ACT.Copy).then_inc(xt_hi, 1)

            squared = [0]

            def sum_squares(src, width, dst):
                if squared[0]:
                    act.wait_ge(sq_done, squared[0])
                squared[0] += 1
                act.activation(junk[:, 0:width], src, ACT.Square, accum_out=dst).then_inc(sq_done, 1)

            split_pair(0)
            for n in range(4):
                xt_upper(n)
                split_pair(n + 1)
            for s in range(SH):
                act.wait_ge(in_x[s], 16)
                sum_squares(xs[:, s, :], D_MODEL, ssq[:, s:s + 1])
            split_pair(5)

            def item(it):
                kind = it[0]
                if kind == "take":
                    j = it[1]
                    g, w = j // 3, j % 3
                    act.wait_ge(blk_done, j * KT + KT)
                    act.wait_ge(rstd_ready, rstd_count["attn"])
                    for s in range(SH):
                        if w < 2:
                            if g:
                                act.wait_ge(rotated, w * 2 + s + 1)
                            dst = qk[:, w, s, :]
                        else:
                            dst = vals[:, g, s, :]
                        act.activation(dst, bank[2 * (j % 2) + s][:], ACT.Copy,
                                       scale=rstd[:, s:s + 1]).then_inc(taken, 1)
                elif kind == "turn":
                    _, g, qk_i, s = it
                    act.wait_ge(b6_full, BANK6[it] + 1)
                    act.activation(qkT[:, g, qk_i, :, s * P:(s + 1) * P],
                                   bank[6][:].rearrange("p (h s) -> p h s", h=HPAIRS), ACT.Copy,
                                   scale=1.0 if qk_i else HEAD_DIM ** -0.5).then_inc(b6_free, 1)
                elif kind == "score":
                    _, g, u = it
                    for t in (2 * u, 2 * u + 1):
                        half, heads, keys = attention_tile(t)
                        T = g * SC_TILES + t
                        act.wait_ge(max_ready, T + 1)
                        for i, head in enumerate(heads):
                            piece = probs[:, T % 4, i * keys:(i + 1) * keys]
                            ins = act.activation(piece, piece, ACT.Exp, bias=neg_max[:, g, half, head:head + 1],
                                                 scale=-1.0, accum_out=sums[:, g, half, head:head + 1])
                        ins.then_inc(exp_done, 1)
                elif kind == "probs" and it[2] % 2 == 0:
                    T = it[1] * SC_TILES + it[2]
                    act.wait_ge(b6_full, BANK6[it] + 1)
                    if T >= 2:
                        act.wait_ge(valued, T - 1)
                    act.activation(probsT[:, T % 2, :], bank[6][:], ACT.Copy).then_inc(b6_free, 1)
                elif kind == "oturn":
                    _, g, s = it
                    n = g * 2 + s
                    sum_squares(o_sb[:, g, s, :], GW, ssq[:, 2 + n:3 + n])
                    act.wait_ge(b6_free, BANK6[it] + 1)
                    act.activation(o_hi[:, g * 4:g * 4 + 4, s * P:(s + 1) * P],
                                   scaled[:, n % 2, :].rearrange("p (k s) -> p k s", k=4), ACT.Copy).then_inc(ot_hi, 1)
                elif kind == "residual" and it[1] >= 2:
                    n = it[1] - 2
                    for s in range(SH):
                        act.wait_ge(res_done, 4 + 2 * n + s + 1)
                        sum_squares(xs[:, s, n * NB:(n + 1) * NB], NB, (ssq2 if n else ssq)[:, 6 + s:7 + s])
                elif kind == "ffnturn":
                    xt_upper(4 + it[1])

            for i in range(FFN0):
                if i % 2:
                    split_pair((i + 11) // 2)
                for it in PLAN.get(i, []):
                    if it[0] == "oturn":
                        act.wait_ge(o_ready, it[1] * 2 + it[2] + 1)
                    item(it)

            def gated(c, done, first):
                act.wait_ge(blk_done, done)
                if first:
                    act.wait_ge(rstd_ready, rstd_count["ffn"])
                for s in range(SH):
                    if not first:
                        act.wait_ge(hid_ready, c * 2 + (s - 1))
                    act.activation(silu[:, s, :], bank[4 + s][:, 0:FC], ACT.Silu,
                                   scale=rstd[:, 6 + s:7 + s]).then_inc(silu_done, 1)

            def hidden_hi(c):
                act.wait_ge(ht_pe, c + 1)
                act.activation(h_hi[:].rearrange("p a s -> p (a s)"), bank[6][:], ACT.Copy).then_inc(ht_hi, 1)

            split_pair(38)
            split_pair(39)
            split_pair(40)
            gated(0, STEP1, True)
            split_pair(41)

            def step(c, pairs):
                def split(m):
                    if m < pairs:
                        split_hi(2 * m, m // 2, c * 32 + 32 * (STEP1 // RING + 1), c * STEP_BLOCKS + (FFN0 - 4 + 2 * m + 2))
                split(0)
                hidden_hi(c - 1)
                split(1)
                split(2)
                gated(c, c * STEP_BLOCKS + (STEP1 - STEP_BLOCKS + GU_BLOCKS), False)
                for m in range(3, 6):
                    split(m)

            with act.Fori(1, NCH - 1) as c:
                step(c, 6)
            step(NCH - 1, 2)
            hidden_hi(NCH - 1)
            for n in range(2):
                for s in range(SH):
                    act.wait_ge(res_done, 8 + 2 * n + s + 1)
                    sum_squares(xs[:, s, n * NB:(n + 1) * NB], NB, (ssq2 if n else ssq)[:, 8 + s:9 + s])

        @block.vector
        def _(dve):
            def split_lo(slot, ready):
                dve.wait_ge(hi_ready, ready)
                dve.tensor_tensor(w_lo[:, slot:slot + 2, :], raw[:, slot:slot + 2, :],
                                  w_hi[:, slot:slot + 2, :].bitcast(f32), ALU.subtract).then_inc(lo_ready, 1)

            def split_pair(p):
                split_lo(2 * p % RING, p + 1)

            def xt_scale(n):
                col = (G_FFN if n >= 4 else G_ATTN) + 2 * (n % 4)
                dve.wait_ge(xt_pe, n + 1)
                if n in (4, 5):
                    dve.wait_ge(ot_lo, n - 1)
                elif n >= 2:
                    dve.wait_ge(xt_lo, n - 1)
                dve.tensor_tensor(scaled[:, n % 2, :].rearrange("p (k s) -> p k s", k=2),
                                  bank[4 + n % 4][:].rearrange("p (k s) -> p k s", k=2),
                                  gain[:, col:col + 2].unsqueeze(2).to_broadcast([P, 2, SEQ]),
                                  ALU.mult).then_inc(xt_gained, 1)

            def xt_lower(n):
                dst = slice(2 * (n % 4), 2 * (n % 4) + 2)
                dve.wait_ge(xt_hi, n + 1)
                dve.tensor_tensor(x_lo[:, dst, :].rearrange("p k s -> p (k s)"), scaled[:, n % 2, :],
                                  x_hi[:, dst, :].bitcast(f32).rearrange("p k s -> p (k s)"),
                                  ALU.subtract).then_inc(xt_lo, 1)

            dve.wait_ge(gain_pe, 1)
            dve.tensor_copy(gain[:], bank[0][:, 0:G_END]).then_inc(gain_ready, 1)
            dve.wait_ge(gain_ready, 1)
            xt_scale(0)
            split_pair(0)
            xt_scale(1)
            xt_lower(0)
            split_pair(1)
            xt_scale(2)
            xt_lower(1)
            split_pair(2)
            xt_scale(3)
            xt_lower(2)
            split_pair(3)
            xt_lower(3)
            split_pair(4)
            split_pair(5)

            def rotate(g, w, s):
                n = g * 4 + w * 2 + s
                src = qk[:, w, s, :].rearrange("p (h d) -> p h d", h=GH)
                swapped = qk[:, w, s, :].rearrange("p (h a d) -> p h a d", h=GH, a=2)[:, :, ::-1, :]
                cos = tab[:, C_COS + s * HEAD_DIM:C_COS + (s + 1) * HEAD_DIM]
                sin = tab[:, C_SIN + s * HEAD_DIM:C_SIN + (s + 1) * HEAD_DIM]
                dve.wait_ge(taken, 2 * (3 * g + w) + s + 1)
                if n:
                    dve.wait_ge(rotated, n)
                dve.tensor_tensor(rope_a[:].rearrange("p (h d) -> p h d", h=GH), src,
                                  cos.unsqueeze(1).to_broadcast([P, GH, HEAD_DIM]), ALU.mult).then_inc(rope_mul, 1)
                dve.tensor_tensor(rope_b[:].rearrange("p (h a d) -> p h a d", h=GH, a=2), swapped,
                                  sin.rearrange("p (a d) -> p a d", a=2).unsqueeze(1)
                                  .to_broadcast([P, GH, 2, HEAD_DIM // 2]), ALU.mult).then_inc(rope_mul, 1)
                dve.wait_ge(rope_mul, 2 * n + 2)
                if g:
                    dve.wait_ge(b6_full, BANK6[("turn", 0, w, s)] + 1)
                dve.tensor_tensor(rot[:, w, s, :], rope_a[:], rope_b[:], ALU.add).then_inc(rotated, 1)

            def item(it):
                kind = it[0]
                if kind == "take" and it[1] % 3 < 2:
                    if it[1] == 0:
                        dve.wait_ge(in_tab, 16)
                    for s in range(SH):
                        rotate(it[1] // 3, it[1] % 3, s)
                elif kind == "score":
                    _, g, u = it
                    dve.wait_ge(scored, g * 3 + u + 1)
                    for t in (2 * u, 2 * u + 1):
                        half, heads, keys = attention_tile(t)
                        T = g * SC_TILES + t
                        if T >= 4:
                            old = (("probs", 0, T - 4) if T - 4 < SC_TILES else ("probs", 1, T - 4 - SC_TILES))
                            dve.wait_ge(b6_full, BANK6[old] + 1)
                        m0 = C_MASK + g * MASK_W + half * P
                        for i, head in enumerate(heads):
                            ins = dve.tensor_tensor_reduce(
                                out=probs[:, T % 4, i * keys:(i + 1) * keys],
                                in0=bank[4 + t % 2][:, i * keys:(i + 1) * keys], in1=tab[:, m0:m0 + keys],
                                scale=-1.0, scalar=3.0e38, op0=ALU.add, op1=ALU.min,
                                accum_out=neg_max[:, g, half, head:head + 1])
                        ins.then_inc(max_ready, 1)
                elif kind == "probs" and it[2] % 2:
                    T = it[1] * SC_TILES + it[2]
                    dve.wait_ge(b6_full, BANK6[it] + 1)
                    if T >= 2:
                        dve.wait_ge(valued, T - 1)
                    dve.tensor_copy(probsT[:, T % 2, :], bank[6][:]).then_inc(b6_free, 1)
                elif kind == "values" and it[2] in (1, SC_TILES - 1):
                    _, g, t = it
                    half = attention_tile(t)[0]
                    n = g * 2 + half
                    dve.wait_ge(exp_done, g * SC_TILES + t + 1)
                    dve.reciprocal(rsums[:, g, half, :], sums[:, g, half, :]).then_inc(rsum_ready, 1)
                    dve.wait_ge(valued, g * SC_TILES + t + 1)
                    dve.wait_ge(rsum_ready, n + 1)
                    dve.tensor_tensor(o_sb[:, g, half, :].rearrange("p (h d) -> p h d", h=GH),
                                      bank[7][:].rearrange("p (h d) -> p h d", h=GH),
                                      rsums[:, g, half, :].unsqueeze(2).to_broadcast([P, GH, HEAD_DIM]),
                                      ALU.mult).then_inc(o_ready, 1)
                elif kind == "oturn":
                    _, g, s = it
                    n = g * 2 + s
                    col = G_MIX + 4 * g
                    dve.wait_ge(b6_full, BANK6[it] + 1)
                    dve.wait_ge(*((ot_lo, n - 1) if n >= 2 else (xt_lo, n + 3)))
                    dve.tensor_tensor(scaled[:, n % 2, :].rearrange("p (k s) -> p k s", k=4),
                                      bank[6][:].rearrange("p (k s) -> p k s", k=4),
                                      gain[:, col:col + 4].unsqueeze(2).to_broadcast([P, 4, P]),
                                      ALU.mult).then_inc(b6_free, 1)
                    dve.wait_ge(ot_hi, n + 1)
                    dve.tensor_tensor(o_lo[:, g * 4:g * 4 + 4, s * P:(s + 1) * P],
                                      scaled[:, n % 2, :].rearrange("p (k s) -> p k s", k=4),
                                      o_hi[:, g * 4:g * 4 + 4, s * P:(s + 1) * P].bitcast(f32),
                                      ALU.subtract).then_inc(ot_lo, 1)
                elif kind == "residual":
                    g, n = it[1] // 2, it[1] % 2
                    dve.wait_ge(blk_done, QKV_BLOCKS + 8 * g + 4 * n + 4)
                    for s in range(SH):
                        dve.wait_ge(rstd_ready, rstd_count[f"o{g}{s}"])
                        if g:
                            dve.wait_ge(res_done, 2 * n + s + 1)
                        cols = xs[:, s, n * NB:(n + 1) * NB]
                        dve.scalar_tensor_tensor(cols, bank[2 * n + s][:], rstd[:, 2 + 2 * g + s:3 + 2 * g + s], cols,
                                                 ALU.mult, ALU.add).then_inc(res_done, 1)
                elif kind == "ffnturn":
                    n = 4 + it[1]
                    xt_scale(n)
                    xt_lower(n)

            for i in range(FFN0):
                if i % 2:
                    split_pair((i + 11) // 2)
                for it in PLAN.get(i, []):
                    item(it)

            def multiply(c):
                for s in range(SH):
                    dve.wait_ge(silu_done, c * 2 + (s + 1))
                    dve.scalar_tensor_tensor(hid[:, s, :], bank[4 + s][:, FC:2 * FC], rstd[:, 6 + s:7 + s],
                                             silu[:, s, :], ALU.mult, ALU.mult).then_inc(hid_ready, 1)

            def hidden_lo(c):
                dve.wait_ge(ht_hi, c + 1)
                dve.tensor_tensor(h_lo[:].rearrange("p a s -> p (a s)"), bank[6][:],
                                  h_hi[:].bitcast(f32).rearrange("p a s -> p (a s)"),
                                  ALU.subtract).then_inc(ht_lo, 1)

            split_pair(38)
            split_pair(39)
            split_pair(40)
            multiply(0)
            split_pair(41)

            def step(c, pairs):
                def split(m):
                    if m < pairs:
                        split_lo(2 * m, c * (STEP_BLOCKS // 2) + (STEP1 // 2 + m + 1))
                split(0)
                hidden_lo(c - 1)
                split(1)
                split(2)
                multiply(c)
                for m in range(3, 6):
                    split(m)

            with dve.Fori(1, NCH - 1) as c:
                step(c, 6)
            step(NCH - 1, 2)
            hidden_lo(NCH - 1)
            dve.wait_ge(blk_done, BLOCKS)
            for n in range(2):
                for s in range(SH):
                    cols = xs[:, s, n * NB:(n + 1) * NB]
                    dve.tensor_tensor(cols, bank[2 * n + s][:], cols, ALU.add).then_inc(res_done, 1)
            dve.wait_ge(in_gout, 16)
            dve.wait_ge(rstd_ready, rstd_count["final"])
            for s in range(SH):
                for n in range(2):
                    cols = xs[:, s, n * NB:(n + 1) * NB]
                    dve.scalar_tensor_tensor(cols, cols, rstd[:, 8 + s:9 + s], gain_out[:, n * NB:(n + 1) * NB],
                                             ALU.mult, ALU.mult).then_inc(fin_ready, 1)

        @block.gpsimd
        def _(pool):
            pool.memset(neg_half[:], -0.5).then_inc(consts_ready, 1)
            pool.wait_ge(consts_ready, 1)
            made = [0]

            def link(ins):
                made[0] += 1
                ins.then_inc(msq_step, 1)
                pool.wait_ge(msq_step, made[0])

            def inverse_rms(cols, width, squares, parts):
                pool.wait_ge(sq_done, squares)
                c = slice(*cols)
                src = ssq[:, c]
                if parts == 2:
                    link(pool.tensor_tensor(ssq[:, c], ssq[:, c], ssq2[:, c], ALU.add))
                link(pool.tensor_scalar(msq[:, c], src, 1.0 / width, EPS, ALU.mult, ALU.add))
                pool.tensor_tensor(rstd[:, c], msq[:, c], neg_half[:, c], ALU.pow).then_inc(rstd_ready, 1)

            inverse_rms((0, 2), D_MODEL, 2, 1)
            for n in range(4):
                inverse_rms((2 + n, 3 + n), GW, 3 + n, 1)
            inverse_rms((6, 8), D_MODEL, 10, 2)
            inverse_rms((8, 10), D_MODEL, 14, 2)


def kernel(**inputs):
    import numpy as np
    import concourse.bacc as bacc
    from concourse.bass_utils import run_bass_kernel_spmd

    table = np.zeros((P, C_END), np.float32)
    table[:, C_ID:C_ID + P] = np.eye(P)
    inv_freq = np.float32(10000.0) ** (-np.arange(0, HEAD_DIM, 2, dtype=np.float32) / np.float32(HEAD_DIM))
    ang = np.arange(SEQ, dtype=np.float32)[:, None] * inv_freq[None, :].astype(np.float32)
    half = HEAD_DIM // 2
    for s in range(SH):
        a = ang[s * P:(s + 1) * P]
        c0, s0 = C_COS + s * HEAD_DIM, C_SIN + s * HEAD_DIM
        table[:, c0:c0 + half] = table[:, c0 + half:c0 + HEAD_DIM] = np.cos(a)
        table[:, s0 + half:s0 + HEAD_DIM] = np.sin(a)
        table[:, s0:s0 + half] = -np.sin(a)
    t, k = np.arange(SEQ)[:, None], np.arange(SEQ)[None, :]
    rel = t - k
    seen = [(rel >= 0).astype(int), sum(((rel >= 0) & (rel <= w) & (rel % d == 0)).astype(int)
                                        for w, d in ((128, 1), (512, 4), (2048, 16)))]
    for g in range(2):
        m = np.where(seen[g] > 0, np.log(np.maximum(seen[g], 1)), -1e30).astype(np.float32)
        m0 = C_MASK + g * MASK_W
        table[:, m0:m0 + P] = m[:P, :P]
        table[:, m0 + P:m0 + MASK_W] = m[P:, :]

    nc = bacc.Bacc("TRN2", target_bir_lowering=False, num_devices=1)
    names = ["x", "w_in", "w_out", "w_gate", "w_up", "w_down", "attn_norm", "moba_out_norm",
             "dil_out_norm", "ffn_norm", "final_norm"]
    arrays, args = {}, []
    for name, a in [(n, np.ascontiguousarray(inputs[n])) for n in names] + [("table", table)]:
        arrays[f"in_{name}"] = a
        args.append(nc.dram_tensor(f"in_{name}", a.shape, mybir.dt.from_np(a.dtype), kind="ExternalInput").ap())
    args.append(nc.dram_tensor("out_0", (1, SEQ, D_MODEL), mybir.dt.float32, kind="ExternalOutput").ap())
    build(nc, *args)
    r = run_bass_kernel_spmd(nc, [arrays], core_ids=[0])
    return r.results[0]["out_0"]
```

```python
import concourse.bass as bass
from concourse import mybir
from contextlib import ExitStack

SEQ, D_MODEL, HEAD_DIM, D_FF = 256, 1024, 64, 2816
EPS = 1e-6
P = 128
SH = SEQ // P
KT = D_MODEL // P
NB = 512
GW = D_MODEL // 2
GH = GW // HEAD_DIM
HPAIRS = GH // 2
RING = 12
QUAD = 4
NQ = RING // QUAD
FC = 256
NCH = D_FF // FC
FT = FC // P
QKV_BLOCKS = 6 * KT
OUT_BLOCKS = KT * D_MODEL // NB
GU_BLOCKS = KT
DOWN_BLOCKS = FT * D_MODEL // NB
STEP_BLOCKS = GU_BLOCKS + DOWN_BLOCKS
FFN0 = QKV_BLOCKS + OUT_BLOCKS
STEP1 = FFN0 + GU_BLOCKS
LAG_HI, LAG_LO = 2, 4
BLOCKS = FFN0 + NCH * STEP_BLOCKS
PAIRS = BLOCKS // 2
HI0, LO0 = (STEP1 + RING - LAG_HI) // 2, (STEP1 + RING - LAG_LO) // 2
SC_TILES = 6

C_ID, C_COS, C_SIN, C_MASK = 0, P, P + SH * HEAD_DIM, P + 2 * SH * HEAD_DIM
MASK_W = P + SEQ
C_END = C_MASK + 2 * MASK_W
G_ATTN, G_MIX, G_FFN, G_END = 0, KT, 2 * KT, 3 * KT

PLAN = {
    7: [("take", 0)],
    12: [("turn", 0, 0, 0)],
    14: [("turn", 0, 0, 1)],
    15: [("take", 1)],
    20: [("turn", 0, 1, 0)],
    21: [("turn", 0, 1, 1)],
    22: [("score", 0, 0)],
    23: [("take", 2)],
    24: [("score", 0, 1)],
    25: [("probs", 0, 0)],
    26: [("probs", 0, 1), ("values", 0, 0)],
    27: [("values", 0, 1), ("score", 0, 2)],
    28: [("probs", 0, 2)],
    29: [("probs", 0, 3), ("values", 0, 2)],
    30: [("values", 0, 3)],
    31: [("probs", 0, 4), ("take", 3)],
    32: [("probs", 0, 5), ("values", 0, 4)],
    33: [("values", 0, 5)],
    34: [("oturn", 0, 0)],
    36: [("turn", 1, 0, 0)],
    37: [("turn", 1, 0, 1)],
    39: [("take", 4), ("oturn", 0, 1)],
    42: [("turn", 1, 1, 0)],
    44: [("turn", 1, 1, 1)],
    45: [("score", 1, 0)],
    47: [("score", 1, 1), ("take", 5)],
    48: [("probs", 1, 0)],
    49: [("probs", 1, 1), ("values", 1, 0)],
    50: [("values", 1, 1), ("score", 1, 2), ("probs", 1, 2)],
    51: [("probs", 1, 3), ("values", 1, 2), ("residual", 0)],
    52: [("values", 1, 3), ("oturn", 1, 0)],
    53: [("probs", 1, 4)],
    54: [("probs", 1, 5), ("values", 1, 4)],
    55: [("values", 1, 5), ("residual", 1), ("oturn", 1, 1)],
    59: [("residual", 2)],
    61: [("ffnturn", 0)],
    62: [("ffnturn", 1)],
    63: [("residual", 3)],
}
STEPS = [(i, item) for i in range(FFN0) for item in PLAN.get(i, [])]
TURNS = [item for _, item in STEPS if item[0] in ("turn", "probs", "oturn")]
BANK6 = {item: n for n, item in enumerate(TURNS)}


def attention_tile(u_tile):
    u, r = u_tile // 2, u_tile % 2
    if u == 0:
        return 0, [2 * i + r for i in range(4)], P
    return 1, [4 * (u - 1) + 2 * i + r for i in range(2)], SEQ


def build(nc, x, x_turned, weights, gains, final_norm, table, out):
    f32, f32r, bf16 = mybir.dt.float32, mybir.dt.float32r, mybir.dt.bfloat16
    ALU, ACT = mybir.AluOpType, mybir.ActivationFunctionType
    ctx = ExitStack()
    with ctx:
        def sb(name, shape, dt=f32):
            return ctx.enter_context(nc.sbuf_tensor(name, shape, dt))

        def sem(name):
            return ctx.enter_context(nc.semaphore(name))

        raw = sb("raw", [P, RING, NB])
        w_hi = sb("w_hi", [P, RING, NB], f32r)
        w_lo = sb("w_lo", [P, RING, NB], f32r)
        xs = sb("xs", [P, SH, D_MODEL])
        tab = sb("tab", [P, C_END])
        gain = sb("gain", [P, G_END])
        xT = sb("xT", [P, KT, SEQ])
        gain_out = sb("gain_out", [P, D_MODEL])
        scaled = sb("scaled", [P, 2, NB])
        x_hi = sb("x_hi", [P, KT, SEQ], f32r)
        x_lo = sb("x_lo", [P, KT, SEQ], f32r)
        o_hi = sb("o_hi", [P, KT, SEQ], f32r)
        o_lo = sb("o_lo", [P, KT, SEQ], f32r)
        qk = sb("qk", [P, 2, SH, GW])
        rot = sb("rot", [P, 2, SH, GW])
        rope_a = sb("rope_a", [P, GW])
        rope_b = sb("rope_b", [P, GW])
        vals = sb("vals", [P, 2, SH, GW])
        qkT = sb("qkT", [P, 2, 2, HPAIRS, SEQ])
        probs = sb("probs", [P, 4, NB])
        probsT = sb("probsT", [P, 2, NB])
        o_sb = sb("o_sb", [P, 2, SH, GW])
        neg_max = sb("neg_max", [P, 2, SH, GH])
        sums = sb("sums", [P, 2, SH, GH])
        rsums = sb("rsums", [P, 2, SH, GH])
        junk = sb("junk", [P, D_MODEL], bf16)
        silu = sb("silu", [P, SH, FC])
        hid = sb("hid", [P, SH, FC])
        h_hi = sb("h_hi", [P, FT * SH, P], f32r)
        h_lo = sb("h_lo", [P, FT * SH, P], f32r)
        ssq = sb("ssq", [P, 10])
        ssq2 = sb("ssq2", [P, 10])
        msq = sb("msq", [P, 10])
        rstd = sb("rstd", [P, 10])
        neg_half = sb("neg_half", [P, 10])

        bank = [ctx.enter_context(nc.psum_tensor(f"bank{i}", [P, NB], f32)) for i in range(8)]
        hidden = (h_hi[:].rearrange("p a s -> p (a s)"), h_lo[:].rearrange("p a s -> p (a s)"))
        hidden_last = (o_hi[:, 0:FT, :].rearrange("p a s -> p (a s)"), o_lo[:, 0:FT, :].rearrange("p a s -> p (a s)"))
        ident = tab[:, C_ID:C_ID + P]

        raw_full = [sem(f"raw_full{i}") for i in range(NQ)]
        in_x = [sem(f"in_x{s}") for s in range(SH)]
        in_xT = [sem(f"in_xT{j}") for j in range(KT // 2)]
        raw_first = sem("raw_first")
        in_gain = sem("in_gain")
        in_ident = sem("in_ident")
        in_tab = sem("in_tab")
        in_gout = sem("in_gout")
        hi_ready = sem("hi_ready")
        lo_ready = sem("lo_ready")
        blk_done = sem("blk_done")
        xt_pe = sem("xt_pe")
        xt_gained = sem("xt_gained")
        xt_hi = sem("xt_hi")
        xt_lo = sem("xt_lo")
        taken = sem("taken")
        rope_mul = sem("rope_mul")
        rotated = sem("rotated")
        b6_full = sem("b6_full")
        b6_free = sem("b6_free")
        scored = sem("scored")
        max_ready = sem("max_ready")
        exp_done = sem("exp_done")
        valued = sem("valued")
        rsum_ready = sem("rsum_ready")
        o_ready = sem("o_ready")
        ot_hi = sem("ot_hi")
        ot_lo = sem("ot_lo")
        sq_done = sem("sq_done")
        consts_ready = sem("consts_ready")
        msq_step = sem("msq_step")
        rstd_ready = sem("rstd_ready")
        res_done = sem("res_done")
        silu_done = sem("silu_done")
        hid_ready = sem("hid_ready")
        ht_pe = sem("ht_pe")
        ht_hi = sem("ht_hi")
        ht_lo = sem("ht_lo")
        fin_ready = sem("fin_ready")
        out_sent = sem("out_sent")

        RSTD_ORDER = ["attn", "o00", "o01", "o10", "o11", "ffn", "final"]
        rstd_count = {n: i + 1 for i, n in enumerate(RSTD_ORDER)}

        block = ctx.enter_context(nc.Block())

        @block.sync
        def _(sp):
            def load_xT(j):
                sp.dma_start(xT[:, 2 * j:2 * j + 2, :], x_turned[:, 2 * j:2 * j + 2, :]).then_inc(in_xT[j], 16)

            def quad(q, pos):
                sp.dma_start(raw[:, pos * QUAD:(pos + 1) * QUAD, :].rearrange("p b n -> p (b n)"),
                             weights[bass.ds(q, 1), :, :].rearrange("q p n -> (q p) n")).then_inc(raw_full[pos], 16)

            load_xT(0)
            sp.dma_start(raw[:, 0:2, :].rearrange("p b n -> p (b n)"), weights[0, :, 0:2 * NB]).then_inc(raw_first, 16)
            load_xT(1)
            sp.dma_start(raw[:, 2:4, :].rearrange("p b n -> p (b n)"),
                         weights[0, :, 2 * NB:4 * NB]).then_inc(raw_full[0], 16)
            load_xT(2)
            quad(1, 1)
            load_xT(3)
            quad(2, 2)
            for s in range(SH):
                sp.dma_start(xs[:, s, :], x[0, s * P:(s + 1) * P, :]).then_inc(in_x[s], 16)
            with sp.Fori(1, BLOCKS // RING) as r:
                for pos in range(NQ):
                    sp.wait_ge(lo_ready, r * (RING // 2) + (2 * pos + 2 - RING // 2))
                    quad(r * NQ + pos, pos)
            for q in range(BLOCKS // RING * NQ, BLOCKS // QUAD):
                sp.wait_ge(lo_ready, 2 * q - 4)
                quad(q, q % NQ)
            for s in range(SH):
                for n in range(2):
                    sp.wait_ge(fin_ready, 2 * s + n + 1)
                    sp.dma_start(out[0, s * P:(s + 1) * P, n * NB:(n + 1) * NB],
                                 xs[:, s, n * NB:(n + 1) * NB]).then_inc(out_sent, 16)
            sp.wait_ge(out_sent, 16 * 2 * SH)

        @block.tensor
        def _(pe):
            def three_pass(dst, a_hi, a_lo, slot, first, last):
                w1, w2 = w_hi[:, slot, :], w_lo[:, slot, :]
                pe.matmul(dst, a_hi, w1, start=first, stop=False)
                pe.matmul(dst, a_hi, w2, start=False, stop=False)
                return pe.matmul(dst, a_lo, w1, start=False, stop=last)

            def x_turn(j):
                dst = bank[4 + j]
                for a in range(2):
                    for s in range(SH):
                        kt = 2 * j + a
                        ins = pe.transpose(dst[:, a * SEQ + s * P:a * SEQ + (s + 1) * P],
                                           xs[:, s, kt * P:(kt + 1) * P], ident)
                ins.then_inc(xt_pe, 1)

            def item(it):
                kind = it[0]
                if kind == "turn":
                    _, g, qk_i, s = it
                    if it == TURNS[0]:
                        pe.wait_ge(in_ident, 16)
                    pe.wait_ge(rotated, g * 4 + qk_i * 2 + s + 1)
                    if BANK6[it]:
                        pe.wait_ge(b6_free, BANK6[it])
                    for p in range(HPAIRS):
                        ins = pe.transpose(bank[6][:, p * P:(p + 1) * P], rot[:, qk_i, s, p * P:(p + 1) * P], ident)
                    ins.then_inc(b6_full, 1)
                elif kind == "score":
                    _, g, u = it
                    pe.wait_ge(b6_free, BANK6[("turn", g, 1, 1)] + 1)
                    done = (g * 3 + u) * 2
                    if done:
                        pe.wait_ge(max_ready, done)
                    half, _, keys = attention_tile(2 * u)
                    for i in range(NB // keys):
                        for r in range(2):
                            head = attention_tile(2 * u + r)[1][i]
                            rows = slice(64 * r, 64 * r + 64)
                            ins = pe.matmul(bank[4 + r][:, i * keys:(i + 1) * keys],
                                            qkT[rows, g, 0, head // 2, half * P:(half + 1) * P],
                                            qkT[rows, g, 1, head // 2, 0:keys], start=True, stop=True)
                    ins.then_inc(scored, 1)
                elif kind == "probs":
                    _, g, t = it
                    T = g * SC_TILES + t
                    pe.wait_ge(exp_done, T + 1)
                    pe.wait_ge(b6_free, BANK6[it])
                    for i in range(NB // P):
                        ins = pe.transpose(bank[6][:, i * P:(i + 1) * P], probs[:, T % 4, i * P:(i + 1) * P], ident)
                    ins.then_inc(b6_full, 1)
                elif kind == "values":
                    _, g, t = it
                    T = g * SC_TILES + t
                    half, heads, keys = attention_tile(t)
                    pe.wait_ge(b6_free, BANK6[("probs", g, t)] + 1)
                    if t == 0:
                        pe.wait_ge(taken, 2 * (3 * g + 2) + 2)
                    if t in (0, 2) and T:
                        pe.wait_ge(o_ready, g * 2 + half)
                    kb = keys // P
                    for i, head in enumerate(heads):
                        for b in range(kb):
                            at = (i * kb + b) * P
                            ins = pe.matmul(bank[7][:, head * HEAD_DIM:(head + 1) * HEAD_DIM],
                                            probsT[:, T % 2, at:at + P],
                                            vals[:, g, b, head * HEAD_DIM:(head + 1) * HEAD_DIM],
                                            start=(b == 0), stop=(b == kb - 1))
                    ins.then_inc(valued, 1)
                elif kind == "oturn":
                    _, g, s = it
                    pe.wait_ge(o_ready, g * 2 + s + 1)
                    pe.wait_ge(b6_free, BANK6[it])
                    for k in range(KT // 2):
                        ins = pe.transpose(bank[6][:, k * P:(k + 1) * P], o_sb[:, g, s, k * P:(k + 1) * P], ident)
                    ins.then_inc(b6_full, 1)
                elif kind == "ffnturn":
                    n = it[1]
                    pe.wait_ge(res_done, 6 + 2 * (n // 2))
                    if n == 2:
                        pe.wait_ge(b6_free, len(TURNS))
                    x_turn(n)

            def qkv_block(i):
                j, k = i // KT, i % KT
                if k % 2 == 0:
                    pe.wait_ge(lo_ready, i // 2 + 1)
                if j == 0:
                    pe.wait_ge(xt_lo, k + 1)
                if j >= 2 and k == 0:
                    pe.wait_ge(taken, 2 * (j - 2) + 2)
                for s in range(SH):
                    cols = slice(s * P, (s + 1) * P)
                    ins = three_pass(bank[2 * (j % 2) + s][:], x_hi[:, k, cols], x_lo[:, k, cols], i % RING,
                                     k == 0, k == KT - 1)
                ins.then_inc(blk_done, 1)

            def out_block(i, s):
                t = i - QKV_BLOCKS
                g, n, kk = t // 8, t // 4 % 2, t % 4
                if s == 0 and kk % 2 == 0:
                    pe.wait_ge(lo_ready, i // 2 + 1)
                if n == 0 and kk == 0:
                    pe.wait_ge(ot_lo, 2 * g + s + 1)
                if kk == 0:
                    if g == 0:
                        pe.wait_ge(taken, 8 + 2 * n + s + 1)
                    else:
                        pe.wait_ge(res_done, 2 * n + s + 1)
                k, cols = g * 4 + kk, slice(s * P, (s + 1) * P)
                ins = three_pass(bank[2 * n + s][:], o_hi[:, k, cols], o_lo[:, k, cols], i % RING, kk == 0, kk == 3)
                if s == SH - 1:
                    ins.then_inc(blk_done, 1)

            for i in range(QKV_BLOCKS):
                qkv_block(i)
                for it in PLAN.get(i, []):
                    item(it)
            for i in range(QKV_BLOCKS, QKV_BLOCKS + OUT_BLOCKS // 2):
                for s in range(SH):
                    out_block(i, s)
                for it in PLAN.get(i, []):
                    item(it)
            for i in range(QKV_BLOCKS + OUT_BLOCKS // 2, FFN0, QUAD):
                for s in range(SH):
                    for b in range(QUAD):
                        out_block(i + b, s)
                        if s == SH - 1:
                            for it in PLAN.get(i + b, []):
                                item(it)

            def gate_up(pair0, k, slot, first_chunk):
                if k % 2 == 0:
                    pe.wait_ge(lo_ready, pair0 + (k // 2 + 1))
                    if first_chunk:
                        pe.wait_ge(xt_lo, KT + k // 2 + 1)
                for s in range(SH):
                    cols = slice(s * P, (s + 1) * P)
                    ins = three_pass(bank[4 + s][:], x_hi[:, k, cols], x_lo[:, k, cols], slot, k == 0, k == KT - 1)
                ins.then_inc(blk_done, 1)

            def turn_hidden(c, c_is_zero):
                pe.wait_ge(hid_ready, c * 2 + 2)
                if c_is_zero:
                    pe.wait_ge(xt_gained, 4)
                else:
                    pe.wait_ge(ht_lo, c)
                for t in range(FT):
                    for s in range(SH):
                        ins = pe.transpose(bank[6][:, (t * SH + s) * P:(t * SH + s + 1) * P],
                                           hid[:, s, t * P:(t + 1) * P], ident)
                ins.then_inc(ht_pe, 1)

            def down(c, pair0, slot0, first, last):
                for t in range(FT):
                    pe.wait_ge(lo_ready, pair0 + (t + 1))
                    if t == 0:
                        pe.wait_ge(ht_lo, c + 1)
                    for n in range(2):
                        for s in range(SH):
                            ins = three_pass(bank[2 * n + s][:], h_hi[:, t * SH + s, :], h_lo[:, t * SH + s, :],
                                             slot0 + 2 * t + n, first and t == 0, False)
                        ins.then_inc(blk_done, 1)
                    if last and t == 0:
                        turn_hidden(NCH - 1, False)

            def step(c, first=False, last=False):
                pair0 = c * (STEP_BLOCKS // 2) + (STEP1 - STEP_BLOCKS) // 2
                pe.wait_ge(hid_ready, c * 2)
                for k in range(KT):
                    gate_up(pair0, k, k, False)
                    if k == 1:
                        turn_hidden(c - 1, first)
                down(c - 1, pair0 + GU_BLOCKS // 2, GU_BLOCKS, first, last)

            pe.wait_ge(xt_gained, 2)
            for k in range(KT):
                gate_up(FFN0 // 2, k, (FFN0 + k) % RING, True)
                if k == 1:
                    item(("ffnturn", 2))
                    item(("ffnturn", 3))
            pe.wait_ge(res_done, 8)
            step(1, first=True)
            with pe.Fori(2, NCH - 1) as c:
                step(c)
            step(NCH - 1, last=True)
            pe.wait_ge(lo_ready, PAIRS)
            pe.wait_ge(ht_lo, NCH)
            for s in range(SH):
                for n in range(2):
                    for t in range(FT):
                        cols = slice((t * SH + s) * P, (t * SH + s + 1) * P)
                        ins = three_pass(bank[2 * n + s][:], hidden_last[0][:, cols], hidden_last[1][:, cols],
                                         2 * t + n, False, t == FT - 1)
                    ins.then_inc(blk_done, 1)

        @block.scalar
        def _(act):
            act.dma_start(gain[:], gains[:, :]).then_inc(in_gain, 16)
            act.dma_start(tab[:, 0:P], table[:, 0:P]).then_inc(in_ident, 16)
            act.dma_start(tab[:, P:C_END], table[:, P:C_END]).then_inc(in_tab, 16)

            def split_hi(slot, pos, quad_round, done):
                if quad_round is not None:
                    act.wait_ge(raw_full[pos], quad_round)
                if done is not None:
                    act.wait_ge(blk_done, done)
                act.activation(w_hi[:, slot:slot + 2, :], raw[:, slot:slot + 2, :], ACT.Copy).then_inc(hi_ready, 1)

            def split_pair(p):
                q = p // 2
                if p == 0:
                    act.wait_ge(raw_first, 16)
                split_hi(2 * p % RING, q % NQ, 16 * (q // NQ + 1) if p else None,
                         2 * p - 10 if p >= RING // 2 else None)

            def xt_upper(n):
                act.wait_ge(xt_gained, n + 1)
                act.activation(x_hi[:, 2 * n:2 * n + 2, :].rearrange("p k s -> p (k s)"),
                               scaled[:, n % 2, :], ACT.Copy).then_inc(xt_hi, 1)

            squared = [0]

            def sum_squares(src, width, dst):
                if squared[0]:
                    act.wait_ge(sq_done, squared[0])
                squared[0] += 1
                act.activation(junk[:, 0:width], src, ACT.Square, accum_out=dst).then_inc(sq_done, 1)

            act.wait_ge(in_gain, 16)
            for n in range(KT // 2):
                act.wait_ge(in_xT[n], 16)
                for k in (2 * n, 2 * n + 1):
                    act.activation(x_hi[:, k, :], xT[:, k, :], ACT.Copy,
                                   scale=gain[:, G_ATTN + k:G_ATTN + k + 1]).then_inc(xt_hi, 1)
                split_pair(n)
            for p in range(KT // 2, (RING - LAG_HI) // 2):
                split_pair(p)
            for s in range(SH):
                act.wait_ge(in_x[s], 16)
                sum_squares(xs[:, s, :], D_MODEL, ssq[:, s:s + 1])

            def residual_squares(n):
                for s in range(SH):
                    act.wait_ge(res_done, 4 + 2 * n + s + 1)
                    sum_squares(xs[:, s, n * NB:(n + 1) * NB], NB, (ssq2 if n else ssq)[:, 6 + s:7 + s])

            def item(it):
                kind = it[0]
                if kind == "take":
                    j = it[1]
                    g, w = j // 3, j % 3
                    act.wait_ge(blk_done, j * KT + KT)
                    act.wait_ge(rstd_ready, rstd_count["attn"])
                    for s in range(SH):
                        if w < 2:
                            if g:
                                act.wait_ge(rotated, w * 2 + s + 1)
                            dst = qk[:, w, s, :]
                        else:
                            dst = vals[:, g, s, :]
                        act.activation(dst, bank[2 * (j % 2) + s][:], ACT.Copy,
                                       scale=rstd[:, s:s + 1]).then_inc(taken, 1)
                elif kind == "turn":
                    _, g, qk_i, s = it
                    act.wait_ge(b6_full, BANK6[it] + 1)
                    act.activation(qkT[:, g, qk_i, :, s * P:(s + 1) * P],
                                   bank[6][:].rearrange("p (h s) -> p h s", h=HPAIRS), ACT.Copy,
                                   scale=1.0 if qk_i else HEAD_DIM ** -0.5).then_inc(b6_free, 1)
                elif kind == "score":
                    _, g, u = it
                    for t in (2 * u, 2 * u + 1):
                        half, heads, keys = attention_tile(t)
                        T = g * SC_TILES + t
                        act.wait_ge(max_ready, T + 1)
                        for i, head in enumerate(heads):
                            piece = probs[:, T % 4, i * keys:(i + 1) * keys]
                            ins = act.activation(piece, piece, ACT.Exp, bias=neg_max[:, g, half, head:head + 1],
                                                 scale=-1.0, accum_out=sums[:, g, half, head:head + 1])
                        ins.then_inc(exp_done, 1)
                elif kind == "oturn":
                    _, g, s = it
                    n = g * 2 + s
                    sum_squares(o_sb[:, g, s, :], GW, ssq[:, 2 + n:3 + n])
                    act.wait_ge(b6_free, BANK6[it] + 1)
                    act.activation(o_hi[:, g * 4:g * 4 + 4, s * P:(s + 1) * P],
                                   scaled[:, n % 2, :].rearrange("p (k s) -> p k s", k=4), ACT.Copy).then_inc(ot_hi, 1)
                elif kind == "residual" and it[1] == 2:
                    residual_squares(0)
                elif kind == "ffnturn":
                    xt_upper(it[1])

            for i in range(FFN0):
                if i % 2:
                    split_pair((i - 1 + RING - LAG_HI) // 2)
                for it in PLAN.get(i, []):
                    if it[0] == "oturn":
                        act.wait_ge(o_ready, it[1] * 2 + it[2] + 1)
                    item(it)

            def gated(c, done, first):
                act.wait_ge(blk_done, done)
                if first:
                    act.wait_ge(rstd_ready, rstd_count["ffn"])
                for s in range(SH):
                    if not first:
                        act.wait_ge(hid_ready, c * 2 + (s - 1))
                    act.activation(silu[:, s, :], bank[4 + s][:, 0:FC], ACT.Silu,
                                   scale=rstd[:, 6 + s:7 + s]).then_inc(silu_done, 1)

            def hidden_hi(c, dst=hidden[0]):
                act.wait_ge(ht_pe, c + 1)
                act.activation(dst, bank[6][:], ACT.Copy).then_inc(ht_hi, 1)

            split_pair(37)
            split_pair(38)
            item(("ffnturn", 2))
            item(("ffnturn", 3))
            residual_squares(1)
            split_pair(39)
            split_pair(40)
            act.dma_start(gain_out[:], final_norm.partition_broadcast(P)).then_inc(in_gout, 16)
            gated(0, STEP1, True)

            def step(c, pairs):
                def split(m):
                    if m < pairs:
                        q = (HI0 + m) // 2
                        split_hi(2 * (HI0 + m) % RING, q % NQ, c * 16 + 16 * (q // NQ),
                                 c * STEP_BLOCKS + (2 * (HI0 + m) - 10 - STEP_BLOCKS))
                split(0)
                hidden_hi(c - 1)
                for m in range(1, 4):
                    split(m)
                gated(c, c * STEP_BLOCKS + (STEP1 - STEP_BLOCKS + GU_BLOCKS), False)
                split(4)
                split(5)

            with act.Fori(1, NCH - 1) as c:
                step(c, 6)
            step(NCH - 1, PAIRS - HI0 - (NCH - 2) * STEP_BLOCKS // 2)
            hidden_hi(NCH - 1, hidden_last[0])
            for s in range(SH):
                for n in range(2):
                    act.wait_ge(res_done, 8 + 2 * s + n + 1)
                    sum_squares(xs[:, s, n * NB:(n + 1) * NB], NB, (ssq2 if n else ssq)[:, 8 + s:9 + s])

        @block.vector
        def _(dve):
            def split_lo(slot, ready):
                dve.wait_ge(hi_ready, ready)
                dve.tensor_tensor(w_lo[:, slot:slot + 2, :], raw[:, slot:slot + 2, :],
                                  w_hi[:, slot:slot + 2, :].bitcast(f32), ALU.subtract).then_inc(lo_ready, 1)

            def split_pair(p):
                split_lo(2 * p % RING, p + 1)

            def xt_scale(n):
                col = G_FFN + 2 * n
                dve.wait_ge(xt_pe, n + 1)
                if n < 2:
                    dve.wait_ge(ot_lo, n + 3)
                else:
                    dve.wait_ge(xt_lo, KT + n - 1)
                dve.tensor_tensor(scaled[:, n % 2, :].rearrange("p (k s) -> p k s", k=2),
                                  bank[4 + n][:].rearrange("p (k s) -> p k s", k=2),
                                  gain[:, col:col + 2].unsqueeze(2).to_broadcast([P, 2, SEQ]),
                                  ALU.mult).then_inc(xt_gained, 1)

            def xt_lower(n):
                dst = slice(2 * n, 2 * n + 2)
                dve.wait_ge(xt_hi, KT + n + 1)
                dve.tensor_tensor(x_lo[:, dst, :].rearrange("p k s -> p (k s)"), scaled[:, n % 2, :],
                                  x_hi[:, dst, :].bitcast(f32).rearrange("p k s -> p (k s)"),
                                  ALU.subtract).then_inc(xt_lo, 1)

            for n in range(KT // 2):
                for k in (2 * n, 2 * n + 1):
                    dve.wait_ge(xt_hi, k + 1)
                    dve.scalar_tensor_tensor(x_lo[:, k, :], xT[:, k, :], gain[:, G_ATTN + k:G_ATTN + k + 1],
                                             x_hi[:, k, :].bitcast(f32), ALU.mult, ALU.subtract).then_inc(xt_lo, 1)
                split_pair(n)

            def rotate(g, w, s):
                n = g * 4 + w * 2 + s
                src = qk[:, w, s, :].rearrange("p (h d) -> p h d", h=GH)
                swapped = qk[:, w, s, :].rearrange("p (h a d) -> p h a d", h=GH, a=2)[:, :, ::-1, :]
                cos = tab[:, C_COS + s * HEAD_DIM:C_COS + (s + 1) * HEAD_DIM]
                sin = tab[:, C_SIN + s * HEAD_DIM:C_SIN + (s + 1) * HEAD_DIM]
                dve.wait_ge(taken, 2 * (3 * g + w) + s + 1)
                if n:
                    dve.wait_ge(rotated, n)
                dve.tensor_tensor(rope_a[:].rearrange("p (h d) -> p h d", h=GH), src,
                                  cos.unsqueeze(1).to_broadcast([P, GH, HEAD_DIM]), ALU.mult).then_inc(rope_mul, 1)
                dve.tensor_tensor(rope_b[:].rearrange("p (h a d) -> p h a d", h=GH, a=2), swapped,
                                  sin.rearrange("p (a d) -> p a d", a=2).unsqueeze(1)
                                  .to_broadcast([P, GH, 2, HEAD_DIM // 2]), ALU.mult).then_inc(rope_mul, 1)
                dve.wait_ge(rope_mul, 2 * n + 2)
                if g:
                    dve.wait_ge(b6_full, BANK6[("turn", 0, w, s)] + 1)
                dve.tensor_tensor(rot[:, w, s, :], rope_a[:], rope_b[:], ALU.add).then_inc(rotated, 1)

            def item(it):
                kind = it[0]
                if kind == "take" and it[1] % 3 < 2:
                    if it[1] == 0:
                        dve.wait_ge(in_tab, 16)
                    for s in range(SH):
                        rotate(it[1] // 3, it[1] % 3, s)
                elif kind == "score":
                    _, g, u = it
                    dve.wait_ge(scored, g * 3 + u + 1)
                    for t in (2 * u, 2 * u + 1):
                        half, heads, keys = attention_tile(t)
                        T = g * SC_TILES + t
                        if T >= 4:
                            old = (("probs", 0, T - 4) if T - 4 < SC_TILES else ("probs", 1, T - 4 - SC_TILES))
                            dve.wait_ge(b6_full, BANK6[old] + 1)
                        m0 = C_MASK + g * MASK_W + half * P
                        for i, head in enumerate(heads):
                            ins = dve.tensor_tensor_reduce(
                                out=probs[:, T % 4, i * keys:(i + 1) * keys],
                                in0=bank[4 + t % 2][:, i * keys:(i + 1) * keys], in1=tab[:, m0:m0 + keys],
                                scale=-1.0, scalar=3.0e38, op0=ALU.add, op1=ALU.min,
                                accum_out=neg_max[:, g, half, head:head + 1])
                        ins.then_inc(max_ready, 1)
                elif kind == "probs":
                    T = it[1] * SC_TILES + it[2]
                    dve.wait_ge(b6_full, BANK6[it] + 1)
                    if T >= 2:
                        dve.wait_ge(valued, T - 1)
                    dve.tensor_copy(probsT[:, T % 2, :], bank[6][:]).then_inc(b6_free, 1)
                elif kind == "values" and it[2] in (1, SC_TILES - 1):
                    _, g, t = it
                    half = attention_tile(t)[0]
                    n = g * 2 + half
                    dve.wait_ge(exp_done, g * SC_TILES + t + 1)
                    dve.reciprocal(rsums[:, g, half, :], sums[:, g, half, :]).then_inc(rsum_ready, 1)
                    dve.wait_ge(valued, g * SC_TILES + t + 1)
                    dve.wait_ge(rsum_ready, n + 1)
                    dve.tensor_tensor(o_sb[:, g, half, :].rearrange("p (h d) -> p h d", h=GH),
                                      bank[7][:].rearrange("p (h d) -> p h d", h=GH),
                                      rsums[:, g, half, :].unsqueeze(2).to_broadcast([P, GH, HEAD_DIM]),
                                      ALU.mult).then_inc(o_ready, 1)
                elif kind == "oturn":
                    _, g, s = it
                    n = g * 2 + s
                    col = G_MIX + 4 * g
                    dve.wait_ge(b6_full, BANK6[it] + 1)
                    if n >= 2:
                        dve.wait_ge(ot_lo, n - 1)
                    dve.tensor_tensor(scaled[:, n % 2, :].rearrange("p (k s) -> p k s", k=4),
                                      bank[6][:].rearrange("p (k s) -> p k s", k=4),
                                      gain[:, col:col + 4].unsqueeze(2).to_broadcast([P, 4, P]),
                                      ALU.mult).then_inc(b6_free, 1)
                    dve.wait_ge(ot_hi, n + 1)
                    dve.tensor_tensor(o_lo[:, g * 4:g * 4 + 4, s * P:(s + 1) * P],
                                      scaled[:, n % 2, :].rearrange("p (k s) -> p k s", k=4),
                                      o_hi[:, g * 4:g * 4 + 4, s * P:(s + 1) * P].bitcast(f32),
                                      ALU.subtract).then_inc(ot_lo, 1)
                elif kind == "residual":
                    g, n = it[1] // 2, it[1] % 2
                    dve.wait_ge(blk_done, QKV_BLOCKS + 8 * g + 4 * n + 4)
                    for s in range(SH):
                        dve.wait_ge(rstd_ready, rstd_count[f"o{g}{s}"])
                        if g:
                            dve.wait_ge(res_done, 2 * n + s + 1)
                        cols = xs[:, s, n * NB:(n + 1) * NB]
                        dve.scalar_tensor_tensor(cols, bank[2 * n + s][:], rstd[:, 2 + 2 * g + s:3 + 2 * g + s], cols,
                                                 ALU.mult, ALU.add).then_inc(res_done, 1)
                elif kind == "ffnturn":
                    xt_scale(it[1])
                    xt_lower(it[1])

            for i in range(FFN0):
                if i % 2:
                    split_pair((i - 1 + RING - LAG_LO) // 2)
                for it in PLAN.get(i, []):
                    item(it)

            def multiply(c):
                for s in range(SH):
                    dve.wait_ge(silu_done, c * 2 + (s + 1))
                    dve.scalar_tensor_tensor(hid[:, s, :], bank[4 + s][:, FC:2 * FC], rstd[:, 6 + s:7 + s],
                                             silu[:, s, :], ALU.mult, ALU.mult).then_inc(hid_ready, 1)

            def hidden_lo(c, parts=hidden):
                dve.wait_ge(ht_hi, c + 1)
                dve.tensor_tensor(parts[1], bank[6][:], parts[0].bitcast(f32), ALU.subtract).then_inc(ht_lo, 1)

            split_pair(36)
            split_pair(37)
            item(("ffnturn", 2))
            item(("ffnturn", 3))
            split_pair(38)
            split_pair(39)
            multiply(0)

            def step(c, pairs):
                def split(m):
                    if m < pairs:
                        split_lo(2 * (LO0 + m) % RING, c * (STEP_BLOCKS // 2) + (LO0 + m + 1 - STEP_BLOCKS // 2))
                split(0)
                hidden_lo(c - 1)
                for m in range(1, 4):
                    split(m)
                multiply(c)
                split(4)
                split(5)

            with dve.Fori(1, NCH - 1) as c:
                step(c, 6)
            step(NCH - 1, PAIRS - LO0 - (NCH - 2) * STEP_BLOCKS // 2)
            hidden_lo(NCH - 1, hidden_last)
            for s in range(SH):
                for n in range(2):
                    cols = xs[:, s, n * NB:(n + 1) * NB]
                    dve.wait_ge(blk_done, BLOCKS - 4 + 2 * s + n + 1)
                    dve.tensor_tensor(cols, bank[2 * n + s][:], cols, ALU.add).then_inc(res_done, 1)
            dve.wait_ge(in_gout, 16)
            for s in range(SH):
                dve.wait_ge(rstd_ready, rstd_count["final"] + s)
                for n in range(2):
                    cols = xs[:, s, n * NB:(n + 1) * NB]
                    dve.scalar_tensor_tensor(cols, cols, rstd[:, 8 + s:9 + s], gain_out[:, n * NB:(n + 1) * NB],
                                             ALU.mult, ALU.mult).then_inc(fin_ready, 1)

        @block.gpsimd
        def _(pool):
            pool.memset(neg_half[:], -0.5).then_inc(consts_ready, 1)
            pool.wait_ge(consts_ready, 1)
            made = [0]

            def link(ins):
                made[0] += 1
                ins.then_inc(msq_step, 1)
                pool.wait_ge(msq_step, made[0])

            def inverse_rms(cols, width, squares, parts):
                pool.wait_ge(sq_done, squares)
                c = slice(*cols)
                src = ssq[:, c]
                if parts == 2:
                    link(pool.tensor_tensor(ssq[:, c], ssq[:, c], ssq2[:, c], ALU.add))
                link(pool.tensor_scalar(msq[:, c], src, 1.0 / width, EPS, ALU.mult, ALU.add))
                pool.tensor_tensor(rstd[:, c], msq[:, c], neg_half[:, c], ALU.pow).then_inc(rstd_ready, 1)

            inverse_rms((0, 2), D_MODEL, 2, 1)
            for n in range(4):
                inverse_rms((2 + n, 3 + n), GW, 3 + n, 1)
            inverse_rms((6, 8), D_MODEL, 10, 2)
            for s in range(SH):
                inverse_rms((8 + s, 9 + s), D_MODEL, 12 + 2 * s, 2)


def kernel(**inputs):
    import numpy as np
    import concourse.bacc as bacc
    from concourse.bass_utils import run_bass_kernel_spmd

    table = np.zeros((P, C_END), np.float32)
    table[:, C_ID:C_ID + P] = np.eye(P)
    inv_freq = np.float32(10000.0) ** (-np.arange(0, HEAD_DIM, 2, dtype=np.float32) / np.float32(HEAD_DIM))
    ang = np.arange(SEQ, dtype=np.float32)[:, None] * inv_freq[None, :].astype(np.float32)
    half = HEAD_DIM // 2
    for s in range(SH):
        a = ang[s * P:(s + 1) * P]
        c0, s0 = C_COS + s * HEAD_DIM, C_SIN + s * HEAD_DIM
        table[:, c0:c0 + half] = table[:, c0 + half:c0 + HEAD_DIM] = np.cos(a)
        table[:, s0 + half:s0 + HEAD_DIM] = np.sin(a)
        table[:, s0:s0 + half] = -np.sin(a)
    t, k = np.arange(SEQ)[:, None], np.arange(SEQ)[None, :]
    rel = t - k
    seen = [(rel >= 0).astype(int), sum(((rel >= 0) & (rel <= w) & (rel % d == 0)).astype(int)
                                        for w, d in ((128, 1), (512, 4), (2048, 16)))]
    for g in range(2):
        m = np.where(seen[g] > 0, np.log(np.maximum(seen[g], 1)), -1e30).astype(np.float32)
        m0 = C_MASK + g * MASK_W
        table[:, m0:m0 + P] = m[:P, :P]
        table[:, m0 + P:m0 + MASK_W] = m[P:, :]

    nc = bacc.Bacc("TRN2", target_bir_lowering=False, num_devices=1)
    get = {n: np.ascontiguousarray(a) for n, a in inputs.items()}

    def quads(w):
        return [np.concatenate(list(w[i:i + QUAD]), axis=1) for i in range(0, len(w), QUAD)]

    loads = []
    for j in range(6):
        c0 = (j % 3) * D_MODEL + (j // 3) * GW
        loads += quads(get["w_in"][:, c0:c0 + NB].reshape(KT, P, NB))
    for g in range(2):
        for n in range(2):
            loads += quads(get["w_out"][g * GW:(g + 1) * GW, n * NB:(n + 1) * NB].reshape(4, P, NB))

    def gate_up(c):
        cols = slice(c * FC, (c + 1) * FC)
        return quads(np.concatenate([get["w_gate"][:, cols], get["w_up"][:, cols]], axis=1).reshape(KT, P, NB))

    def down(c):
        w = get["w_down"][c * FC:(c + 1) * FC].reshape(FT, P, 2, NB).transpose(0, 2, 1, 3)
        return quads(w.reshape(FT * 2, P, NB))

    loads += gate_up(0)
    for c in range(1, NCH):
        loads += gate_up(c) + down(c - 1)
    loads += down(NCH - 1)
    x = get["x"]
    x_turned = x[0].T.reshape(KT, P, SEQ).transpose(1, 0, 2)
    gains = np.concatenate([get[n].reshape(-1, P) for n in ("attn_norm", "moba_out_norm", "dil_out_norm",
                                                            "ffn_norm")]).T
    arrays, args = {}, []
    for name, a in (("x", x), ("x_turned", x_turned), ("weights", np.stack(loads)), ("gains", gains),
                    ("final_norm", get["final_norm"]), ("table", table)):
        a = arrays[f"in_{name}"] = np.ascontiguousarray(a)
        args.append(nc.dram_tensor(f"in_{name}", a.shape, mybir.dt.from_np(a.dtype), kind="ExternalInput").ap())
    args.append(nc.dram_tensor("out_0", (1, SEQ, D_MODEL), mybir.dt.float32, kind="ExternalOutput").ap())
    build(nc, *args)
    r = run_bass_kernel_spmd(nc, [arrays], core_ids=[0])
    return r.results[0]["out_0"]
```

```python
import concourse.bass as bass
from concourse import mybir
from contextlib import ExitStack

SEQ, D_MODEL, HEAD_DIM, D_FF = 256, 1024, 64, 2816
EPS = 1e-6
MEAN_SCALE = D_MODEL ** -0.5
P = 128
SH = SEQ // P
KT = D_MODEL // P
NB = 512
GW = D_MODEL // 2
GH = GW // HEAD_DIM
HPAIRS = GH // 2
WARM = 10
SINGLES = KT
RING = 12
QUAD = 4
NQ = RING // QUAD
FC = 256
NCH = D_FF // FC
FT = FC // P
QKV_BLOCKS = 6 * KT
OUT_BLOCKS = KT * D_MODEL // NB
GU_BLOCKS = KT
DOWN_BLOCKS = FT * D_MODEL // NB
STEP_BLOCKS = GU_BLOCKS + DOWN_BLOCKS
FFN0 = QKV_BLOCKS + OUT_BLOCKS
STEP1 = FFN0 + GU_BLOCKS
LAG_HI, LAG_LO = 2, 4
BLOCKS = FFN0 + NCH * STEP_BLOCKS
PAIRS = BLOCKS // 2
HI0, LO0 = (STEP1 + RING - LAG_HI) // 2, (STEP1 + RING - LAG_LO) // 2
EARLY_HI = (RING + QUAD) // 2
FIRST_LOADS = {0: 1, 1: 1, 2: 2, 4: 2, 6: 2, 8: 2, 10: 2}
TURN_BANK = (4, 5), (4, 7)
SC_TILES = 6

C_ID, C_ROPE, C_MASK = 0, P, P + 2 * SH * HEAD_DIM
MASK_W = P + SEQ
C_END = C_MASK + 2 * MASK_W
G_ATTN, G_MIX, G_FFN, G_END = 0, KT, 2 * KT, 3 * KT

PLAN = {
    9: [("rope", 0, 0)],
    11: [("rope", 0, 1)],
    15: [("turn", 0, 0, 0), ("rope", 1, 0)],
    16: [("turn", 0, 0, 1)],
    17: [("rope", 1, 1)],
    20: [("turn", 0, 1, 0)],
    21: [("turn", 0, 1, 1)],
    22: [("score", 0, 0)],
    25: [("probs", 0, 0), ("take", 2)],
    26: [("score", 0, 1), ("probs", 0, 1)],
    27: [("values", 0, 0), ("probs", 0, 2)],
    28: [("score", 0, 2)],
    29: [("values", 0, 1), ("probs", 0, 3)],
    30: [("values", 0, 2), ("probs", 0, 4)],
    31: [("values", 0, 3), ("rope", 3, 0), ("values", 0, 4), ("probs", 0, 5)],
    32: [("values", 0, 5), ("oturn", 0, 0)],
    33: [("rope", 3, 1)],
    35: [("oturn", 0, 1)],
    37: [("turn", 1, 0, 0), ("turn", 1, 0, 1)],
    40: [("rope", 4, 0)],
    41: [("rope", 4, 1)],
    43: [("turn", 1, 1, 0)],
    44: [("turn", 1, 1, 1), ("score", 1, 0)],
    47: [("probs", 1, 0), ("take", 5), ("score", 1, 1)],
    49: [("probs", 1, 1), ("score", 1, 2), ("values", 1, 0), ("probs", 1, 2)],
    50: [("values", 1, 1), ("probs", 1, 3), ("residual", 0)],
    51: [("values", 1, 2), ("probs", 1, 4)],
    52: [("values", 1, 3), ("oturn", 1, 0)],
    53: [("probs", 1, 5)],
    54: [("values", 1, 4), ("values", 1, 5)],
    55: [("oturn", 1, 1)],
    56: [("residual", 1)],
    59: [("residual", 2)],
    60: [("ffnturn", 0), ("ffnturn", 1), ("residual", 3)],
}
STEPS = [(i, item) for i in range(FFN0) for item in PLAN.get(i, [])]
BANK6 = {item: n for n, item in enumerate(item for _, item in STEPS if item[0] in ("probs", "oturn"))}


def attention_tile(u_tile):
    u, r = u_tile // 2, u_tile % 2
    if u == 0:
        return 0, [2 * i + r for i in range(4)], P
    return 1, [4 * (u - 1) + 2 * i + r for i in range(2)], SEQ


def build(nc, x, x_turned, weights, gains, final_norm, table, out):
    f32, f32r, bf16 = mybir.dt.float32, mybir.dt.float32r, mybir.dt.bfloat16
    ALU, ACT = mybir.AluOpType, mybir.ActivationFunctionType
    ctx = ExitStack()
    with ctx:
        def sb(name, shape, dt=f32):
            return ctx.enter_context(nc.sbuf_tensor(name, shape, dt))

        def sem(name):
            return ctx.enter_context(nc.semaphore(name))

        raw = sb("raw", [P, RING, NB])
        w_hi = sb("w_hi", [P, RING, NB], f32r)
        w_lo = sb("w_lo", [P, RING, NB], f32r)
        xs = sb("xs", [P, SH, D_MODEL])
        tab = sb("tab", [P, C_END])
        gain = sb("gain", [P, G_END])
        gain_out = sb("gain_out", [P, D_MODEL])
        scaled = sb("scaled", [P, 2, NB])
        x_hi = sb("x_hi", [P, KT, SEQ], f32r)
        x_lo = sb("x_lo", [P, KT, SEQ], f32r)
        o_hi = sb("o_hi", [P, KT, SEQ], f32r)
        o_lo = sb("o_lo", [P, KT, SEQ], f32r)
        rot = sb("rot", [P, 2, SH, GW])
        rotary = sb("rotary", [P, SH, 2 * HEAD_DIM])
        rope_a = sb("rope_a", [P, GW])
        rope_b = sb("rope_b", [P, GW])
        vals = sb("vals", [P, 2, SH, GW])
        qkT_hi = sb("qkT_hi", [P, 2, HPAIRS, SEQ], f32r)
        qkT_lo = sb("qkT_lo", [P, 2, HPAIRS, SEQ], f32r)
        qkT_first = sb("qkT_first", [P, 2, HPAIRS, P])
        probs = sb("probs", [P, 4, NB])
        probsT = sb("probsT", [P, 2, NB])
        o_sb = sb("o_sb", [P, 2, SH, GW])
        normed = rot[:]
        xT = o_sb[:].rearrange("p g s (a t) -> p (g s a) t", t=SEQ)
        neg_max = sb("neg_max", [P, 2, SH, GH])
        sums = sb("sums", [P, 2, SH, GH])
        rsums = sb("rsums", [P, 2, SH, GH])
        warm = sb("warm", [P, NB], bf16)
        warm_out = sb("warm_out", [P, 2])
        junk = sb("junk", [P, D_MODEL], bf16)
        silu = sb("silu", [P, SH, FC])
        hid = sb("hid", [P, SH, FC])
        h_hi = sb("h_hi", [P, FT * SH, P], f32r)
        h_lo = sb("h_lo", [P, FT * SH, P], f32r)
        ssq = sb("ssq", [P, 10])
        ssq2 = sb("ssq2", [P, 10])
        msq = sb("msq", [P, 10])
        rstd = sb("rstd", [P, 10])
        neg_half = sb("neg_half", [P, 10])

        bank = [ctx.enter_context(nc.psum_tensor(f"bank{i}", [P, NB], f32)) for i in range(8)]
        hidden = (h_hi[:].rearrange("p a s -> p (a s)"), h_lo[:].rearrange("p a s -> p (a s)"))
        hidden_last = (o_hi[:, 0:FT, :].rearrange("p a s -> p (a s)"), o_lo[:, 0:FT, :].rearrange("p a s -> p (a s)"))
        ident = tab[:, C_ID:C_ID + P]

        raw_full = [sem(f"raw_full{i}") for i in range(NQ)]
        in_x = [sem(f"in_x{s}") for s in range(SH)]
        in_xT = [sem(f"in_xT{j}") for j in range(KT // 2)]
        first_sem = {b: raw_full[b // QUAD] if (b + n) % QUAD == 0 else sem(f"raw_first{b}")
                     for b, n in FIRST_LOADS.items()}
        in_gain = sem("in_gain")
        warm_ready = sem("warm_ready")
        in_tab = sem("in_tab")
        in_mask = sem("in_mask")
        in_gout = sem("in_gout")
        hi_ready = sem("hi_ready")
        lo_ready = sem("lo_ready")
        hi_single = sem("hi_single")
        lo_single = sem("lo_single")
        blk_done = sem("blk_done")
        xt_pe = sem("xt_pe")
        xt_hi = sem("xt_hi")
        xt_lo = sem("xt_lo")
        v_taken = sem("v_taken")
        rotary_ready = sem("rotary_ready")
        rope_mul = sem("rope_mul")
        rotated = sem("rotated")
        b6_full = sem("b6_full")
        b6_free = sem("b6_free")
        turned = sem("turned")
        qk_first = sem("qk_first")
        qk_lo = sem("qk_lo")
        qk_hi = sem("qk_hi")
        scored = sem("scored")
        max_ready = sem("max_ready")
        exp_done = sem("exp_done")
        valued = sem("valued")
        rsum_ready = sem("rsum_ready")
        o_ready = sem("o_ready")
        ot_hi = sem("ot_hi")
        ot_lo = sem("ot_lo")
        sq_done = sem("sq_done")
        consts_ready = sem("consts_ready")
        msq_step = sem("msq_step")
        rstd_ready = sem("rstd_ready")
        res_done = sem("res_done")
        gu_half = sem("gu_half")
        silu_done = sem("silu_done")
        hid_ready = sem("hid_ready")
        ht_pe = sem("ht_pe")
        ht_hi = sem("ht_hi")
        ht_lo = sem("ht_lo")
        gained = sem("gained")
        fin_ready = sem("fin_ready")
        fin_dve = sem("fin_dve")
        out_sent = sem("out_sent")

        RSTD_ORDER = ["attn", "o00", "o01", "o10", "o11", "ffn", "final"]
        rstd_count = {n: i + 1 for i, n in enumerate(RSTD_ORDER)}

        block = ctx.enter_context(nc.Block())

        @block.sync
        def _(sp):
            def load_xT(j):
                sp.dma_start(xT[:, 2 * j:2 * j + 2, :], x_turned[:, 2 * j:2 * j + 2, :]).then_inc(in_xT[j], 16)

            def quad(q, pos):
                sp.dma_start(raw[:, pos * QUAD:(pos + 1) * QUAD, :].rearrange("p b n -> p (b n)"),
                             weights[bass.ds(q, 1), :, :].rearrange("q p n -> (q p) n")).then_inc(raw_full[pos], 16)

            load_xT(0)
            for b, full in FIRST_LOADS.items():
                n = b % QUAD
                sp.dma_start(raw[:, b:b + full, :].rearrange("p b n -> p (b n)"),
                             weights[b // QUAD, :, n * NB:(n + full) * NB]).then_inc(first_sem[b], 16)
                if b in (1, 2, 4):
                    load_xT((1, 2, 4).index(b) + 1)
            sp.wait_ge(lo_ready, 2)
            quad(NQ, 0)
            for s in range(SH):
                sp.dma_start(xs[:, s, :], x[0, s * P:(s + 1) * P, :]).then_inc(in_x[s], 16)
            sp.dma_start(tab[:, 0:C_MASK], table[:, 0:C_MASK]).then_inc(in_tab, 16)
            for pos in range(1, NQ):
                sp.wait_ge(lo_ready, 2 * pos + 2)
                quad(NQ + pos, pos)
            sp.dma_start(tab[:, C_MASK:C_END], table[:, C_MASK:C_END]).then_inc(in_mask, 16)
            with sp.Fori(2, BLOCKS // RING) as r:
                for pos in range(NQ):
                    sp.wait_ge(lo_ready, r * (RING // 2) + (2 * pos + 2 - RING // 2))
                    quad(r * NQ + pos, pos)
            for q in range(BLOCKS // RING * NQ, BLOCKS // QUAD):
                sp.wait_ge(lo_ready, 2 * q - 4)
                quad(q, q % NQ)
            for s in range(SH):
                for n in range(2):
                    sp.wait_ge(*((fin_dve, 1) if (s, n) == (1, 0) else (fin_ready, s + n + 1)))
                    sp.dma_start(out[0, s * P:(s + 1) * P, n * NB:(n + 1) * NB],
                                 normed[:, s, n, :]).then_inc(out_sent, 16)
            sp.wait_ge(out_sent, 16 * 2 * SH)

        @block.tensor
        def _(pe):
            def three_pass(dst, a_hi, a_lo, slot, first, last):
                w1, w2 = w_hi[:, slot, :], w_lo[:, slot, :]
                pe.matmul(dst, a_hi, w1, start=first, stop=False)
                pe.matmul(dst, a_hi, w2, start=False, stop=False)
                return pe.matmul(dst, a_lo, w1, start=False, stop=last)

            def x_turn(j):
                dst = bank[4 + j]
                for a in range(2):
                    for s in range(SH):
                        kt = 2 * j + a
                        ins = pe.transpose(dst[:, a * SEQ + s * P:a * SEQ + (s + 1) * P],
                                           xs[:, s, kt * P:(kt + 1) * P], ident)
                ins.then_inc(xt_pe, 1)

            def item(it):
                kind = it[0]
                if kind == "turn":
                    _, g, qk_i, s = it
                    n = g * 4 + qk_i * 2 + s
                    if n == 0:
                        pe.wait_ge(in_tab, 16)
                    pe.wait_ge(rotated, n + 1)
                    if (qk_i, s) == (1, 0):
                        pe.wait_ge(qk_first, 2 * g + 1)
                    elif g:
                        pe.wait_ge(*((o_ready, 2 * g) if qk_i else (max_ready, SC_TILES)))
                    for p in range(HPAIRS):
                        ins = pe.transpose(bank[TURN_BANK[qk_i][s]][:, p * P:(p + 1) * P], rot[:, qk_i, s, p * P:(p + 1) * P], ident)
                    ins.then_inc(turned, 1)
                elif kind == "score":
                    _, g, u = it
                    pe.wait_ge(*((qk_lo, g * 4 + 4) if u else (qk_first, 2 * g + 2)))
                    done = (g * 3 + u) * 2
                    if done:
                        pe.wait_ge(max_ready, done)
                    half, _, keys = attention_tile(2 * u)
                    for i in range(NB // keys):
                        for r in range(2):
                            head = attention_tile(2 * u + r)[1][i]
                            rows = slice(64 * r, 64 * r + 64)
                            dst = bank[4 + r][:, i * keys:(i + 1) * keys]
                            q_at = (rows, 0, head // 2, slice(half * P, (half + 1) * P))
                            k_at = (rows, 1, head // 2, slice(0, keys))
                            if u == 0:
                                ins = pe.matmul(dst, qkT_first[rows, 0, head // 2, :],
                                                qkT_first[rows, 1, head // 2, :], start=True, stop=True)
                                continue
                            pe.matmul(dst, qkT_hi[q_at], qkT_hi[k_at], start=True, stop=False)
                            pe.matmul(dst, qkT_hi[q_at], qkT_lo[k_at], start=False, stop=False)
                            ins = pe.matmul(dst, qkT_lo[q_at], qkT_hi[k_at], start=False, stop=True)
                    ins.then_inc(scored, 1)
                elif kind == "probs":
                    _, g, t = it
                    T = g * SC_TILES + t
                    pe.wait_ge(exp_done, T + 1)
                    if BANK6[it]:
                        pe.wait_ge(b6_free, BANK6[it])
                    for i in range(NB // P):
                        ins = pe.transpose(bank[6][:, i * P:(i + 1) * P], probs[:, T % 4, i * P:(i + 1) * P], ident)
                    ins.then_inc(b6_full, 1)
                elif kind == "values":
                    _, g, t = it
                    T = g * SC_TILES + t
                    half, heads, keys = attention_tile(t)
                    pe.wait_ge(b6_free, BANK6[("probs", g, t)] + 1)
                    if t == 0:
                        pe.wait_ge(qk_lo, g * 4 + 4)
                        pe.wait_ge(v_taken, 2 * g + 2)
                    if t in (0, 2) and T:
                        pe.wait_ge(o_ready, g * 2 + half)
                    kb = keys // P
                    for i, head in enumerate(heads):
                        for b in range(kb):
                            at = (i * kb + b) * P
                            ins = pe.matmul(bank[7][:, head * HEAD_DIM:(head + 1) * HEAD_DIM],
                                            probsT[:, T % 2, at:at + P],
                                            vals[:, g, b, head * HEAD_DIM:(head + 1) * HEAD_DIM],
                                            start=(b == 0), stop=(b == kb - 1))
                    ins.then_inc(valued, 1)
                elif kind == "oturn":
                    _, g, s = it
                    pe.wait_ge(o_ready, g * 2 + s + 1)
                    pe.wait_ge(b6_free, BANK6[it])
                    for k in range(KT // 2):
                        ins = pe.transpose(bank[6][:, k * P:(k + 1) * P], o_sb[:, g, s, k * P:(k + 1) * P], ident)
                    ins.then_inc(b6_full, 1)
                elif kind == "ffnturn":
                    n = it[1]
                    pe.wait_ge(res_done, 6 + 2 * (n // 2))
                    if n == 2:
                        pe.wait_ge(b6_free, len(BANK6))
                    x_turn(n)

            def qkv_block(i):
                j, k = i // KT, i % KT
                if i < SINGLES:
                    pe.wait_ge(*((lo_ready, i // 2 + 1) if i % 2 else (lo_single, i // 2 + 1)))
                elif k % 2 == 0:
                    pe.wait_ge(lo_ready, i // 2 + 1)
                if j == 0:
                    pe.wait_ge(xt_lo, k + 1)
                if j >= 2 and k == 0:
                    g, w = (j - 2) // 3, (j - 2) % 3
                    pe.wait_ge(*((v_taken, 2 * g + 2) if w == 2 else (rope_mul, 8 * g + 4 * w + 4)))
                for s in range(SH):
                    cols = slice(s * P, (s + 1) * P)
                    ins = three_pass(bank[2 * (j % 2) + s][:], x_hi[:, k, cols], x_lo[:, k, cols], i % RING,
                                     k == 0, k == KT - 1)
                ins.then_inc(blk_done, 1)

            def out_block(i, s):
                t = i - QKV_BLOCKS
                g, n, kk = t // 8, t // 4 % 2, t % 4
                if s == 0 and kk % 2 == 0:
                    pe.wait_ge(lo_ready, i // 2 + 1)
                if n == 0 and kk == 0:
                    pe.wait_ge(ot_lo, 2 * g + s + 1)
                if kk == 0:
                    if g == 0:
                        pe.wait_ge(*((v_taken, 2 + s + 1) if n else (rope_mul, 12 + 2 * s + 2)))
                    else:
                        pe.wait_ge(res_done, 2 * n + s + 1)
                k, cols = g * 4 + kk, slice(s * P, (s + 1) * P)
                ins = three_pass(bank[2 * n + s][:], o_hi[:, k, cols], o_lo[:, k, cols], i % RING, kk == 0, kk == 3)
                if s == SH - 1:
                    ins.then_inc(blk_done, 1)

            pe.wait_ge(warm_ready, 1)
            for _ in range(WARM):
                pe.matmul(bank[7][:], warm[:, 0:P], warm[:], start=True, stop=True)
            for i in range(QKV_BLOCKS):
                qkv_block(i)
                for it in PLAN.get(i, []):
                    item(it)
            for i in range(QKV_BLOCKS, QKV_BLOCKS + OUT_BLOCKS // 2):
                for s in range(SH):
                    out_block(i, s)
                for it in PLAN.get(i, []):
                    item(it)
            for i in range(QKV_BLOCKS + OUT_BLOCKS // 2, FFN0, QUAD):
                for s in range(SH):
                    for b in range(QUAD):
                        out_block(i + b, s)
                        if s == SH - 1:
                            for it in PLAN.get(i + b, []):
                                item(it)

            def gate_up(k, s, slot):
                cols = slice(s * P, (s + 1) * P)
                ins = three_pass(bank[4 + s][:], x_hi[:, k, cols], x_lo[:, k, cols], slot, k == 0, k == KT - 1)
                if s == SH - 1:
                    ins.then_inc(blk_done, 1)
                elif k == KT - 1:
                    ins.then_inc(gu_half, 1)

            def turn_hidden(c, c_is_zero):
                pe.wait_ge(hid_ready, c * 2 + 2)
                if c_is_zero:
                    pe.wait_ge(xt_lo, 2 * KT)
                else:
                    pe.wait_ge(ht_lo, c)
                for t in range(FT):
                    for s in range(SH):
                        ins = pe.transpose(bank[6][:, (t * SH + s) * P:(t * SH + s + 1) * P],
                                           hid[:, s, t * P:(t + 1) * P], ident)
                ins.then_inc(ht_pe, 1)

            def down(c, pair0, slot0, first, last):
                for t in range(FT):
                    pe.wait_ge(lo_ready, pair0 + (t + 1))
                    if t == 0:
                        pe.wait_ge(ht_lo, c + 1)
                    for n in range(2):
                        for s in range(SH):
                            ins = three_pass(bank[2 * n + s][:], h_hi[:, t * SH + s, :], h_lo[:, t * SH + s, :],
                                             slot0 + 2 * t + n, first and t == 0, False)
                        ins.then_inc(blk_done, 1)
                    if last and t == 0:
                        turn_hidden(NCH - 1, False)

            def step(c, first=False, last=False):
                pair0 = c * (STEP_BLOCKS // 2) + (STEP1 - STEP_BLOCKS) // 2
                for h in range(2):
                    for s in range(SH):
                        if h == 0:
                            pe.wait_ge(hid_ready, c * 2 + (s - 1))
                        for k in range(QUAD * h, QUAD * h + QUAD):
                            if s == 0 and k % 2 == 0:
                                pe.wait_ge(lo_ready, pair0 + (k // 2 + 1))
                            gate_up(k, s, k)
                    if h == 0:
                        turn_hidden(c - 1, first)
                down(c - 1, pair0 + GU_BLOCKS // 2, GU_BLOCKS, first, last)

            def first_chunk(k, s):
                if s == 0:
                    if k % 2 == 0:
                        pe.wait_ge(lo_ready, FFN0 // 2 + k // 2 + 1)
                    pe.wait_ge(xt_lo, KT + k + 1)
                if k == 0 and s == 1:
                    pe.wait_ge(xt_lo, KT + 4)
                gate_up(k, s, (FFN0 + k) % RING)

            pe.wait_ge(xt_lo, KT + 2)
            for k in range(QUAD):
                for s in range(SH):
                    first_chunk(k, s)
                if k == 1:
                    item(("ffnturn", 2))
                    item(("ffnturn", 3))
            for s in range(SH):
                for k in range(QUAD, KT):
                    first_chunk(k, s)
            pe.wait_ge(res_done, 8)
            step(1, first=True)
            with pe.Fori(2, NCH - 1) as c:
                step(c)
            step(NCH - 1, last=True)
            pe.wait_ge(lo_ready, PAIRS)
            pe.wait_ge(ht_lo, NCH)
            for s in range(SH):
                for n in range(2):
                    for t in range(FT):
                        cols = slice((t * SH + s) * P, (t * SH + s + 1) * P)
                        ins = three_pass(bank[2 * n + s][:], hidden_last[0][:, cols], hidden_last[1][:, cols],
                                         2 * t + n, False, t == FT - 1)
                    ins.then_inc(blk_done, 1)

        @block.scalar
        def _(act):
            act.dma_start(gain[:], gains[:, :]).then_inc(in_gain, 16)
            act.wait_ge(warm_ready, 1)
            act.activation(warm_out[:, 0:1], warm[:, 0:1], ACT.Exp)

            def split_hi(slot, pos, quad_round, done):
                if quad_round is not None:
                    act.wait_ge(raw_full[pos], quad_round)
                if done is not None:
                    act.wait_ge(blk_done, done)
                act.activation(w_hi[:, slot:slot + 2, :], raw[:, slot:slot + 2, :], ACT.Copy).then_inc(hi_ready, 1)

            def split_single(b):
                if b in first_sem:
                    act.wait_ge(first_sem[b], 16)
                act.activation(w_hi[:, b, :], raw[:, b, :], ACT.Copy).then_inc(hi_ready if b % 2 else hi_single, 1)

            def split_pair(p):
                q = p // 2
                if p < RING // 2:
                    act.wait_ge(first_sem[2 * p], 16)
                    split_hi(2 * p, None, None, None)
                else:
                    split_hi(2 * p % RING, q % NQ, 16 * (q // NQ + 1), 2 * p - 10)

            def ffn_turn(n):
                act.wait_ge(xt_pe, n + 1)
                for a in range(2):
                    k = 2 * n + a
                    act.activation(x_hi[:, k, :], bank[4 + n][:, a * SEQ:(a + 1) * SEQ], ACT.Copy,
                                   scale=gain[:, G_FFN + k:G_FFN + k + 1]).then_inc(xt_hi, 1)

            squared = [0]

            def sum_squares(src, width, dst, scale=1.0):
                if squared[0]:
                    act.wait_ge(sq_done, squared[0])
                squared[0] += 1
                act.activation(junk[:, 0:width], src, ACT.Square, scale=scale,
                               accum_out=dst).then_inc(sq_done, 1)

            act.wait_ge(in_gain, 16)
            for k in range(KT):
                if k % 2 == 0:
                    act.wait_ge(in_xT[k // 2], 16)
                act.activation(x_hi[:, k, :], xT[:, k, :], ACT.Copy,
                               scale=gain[:, G_ATTN + k:G_ATTN + k + 1]).then_inc(xt_hi, 1)
                split_single(k)
            for p in range(SINGLES // 2, EARLY_HI):
                split_pair(p)
            for s in range(SH):
                act.wait_ge(in_x[s], 16)
                sum_squares(xs[:, s, :], D_MODEL, ssq[:, s:s + 1])

            def residual_squares(n):
                for s in range(SH):
                    act.wait_ge(res_done, 4 + 2 * n + s + 1)
                    sum_squares(xs[:, s, n * NB:(n + 1) * NB], NB, (ssq2 if n else ssq)[:, 6 + s:7 + s],
                                MEAN_SCALE)

            def item(it):
                kind = it[0]
                if kind == "take":
                    j = it[1]
                    g = j // 3
                    act.wait_ge(blk_done, j * KT + KT)
                    act.wait_ge(rstd_ready, rstd_count["attn"])
                    for s in range(SH):
                        act.activation(vals[:, g, s, :], bank[2 * (j % 2) + s][:], ACT.Copy,
                                       scale=rstd[:, s:s + 1]).then_inc(v_taken, 1)
                elif kind == "turn":
                    _, g, qk_i, s = it
                    act.wait_ge(turned, g * 4 + qk_i * 2 + s + 1)
                    if g:
                        act.wait_ge(scored, 3)
                    src = bank[TURN_BANK[qk_i][s]][:].rearrange("p (h s) -> p h s", h=HPAIRS)
                    scale = 1.0 if qk_i else HEAD_DIM ** -0.5
                    if s == 0:
                        act.activation(qkT_first[:, qk_i, :, :], src, ACT.Copy, scale=scale).then_inc(qk_first, 1)
                        act.wait_ge(qk_first, 2 * g + qk_i + 1)
                        src, scale = qkT_first[:, qk_i, :, :], 1.0
                    act.activation(qkT_hi[:, qk_i, :, s * P:(s + 1) * P], src, ACT.Copy, scale=scale).then_inc(qk_hi, 1)
                elif kind == "score":
                    _, g, u = it
                    for t in (2 * u, 2 * u + 1):
                        half, heads, keys = attention_tile(t)
                        T = g * SC_TILES + t
                        act.wait_ge(max_ready, T + 1)
                        for i, head in enumerate(heads):
                            piece = probs[:, T % 4, i * keys:(i + 1) * keys]
                            ins = act.activation(piece, piece, ACT.Exp, bias=neg_max[:, g, half, head:head + 1],
                                                 scale=-1.0, accum_out=sums[:, g, half, head:head + 1])
                        ins.then_inc(exp_done, 1)
                elif kind == "oturn":
                    _, g, s = it
                    n = g * 2 + s
                    sum_squares(o_sb[:, g, s, :], GW, ssq[:, 2 + n:3 + n])
                    act.wait_ge(b6_free, BANK6[it] + 1)
                    act.activation(o_hi[:, g * 4:g * 4 + 4, s * P:(s + 1) * P],
                                   scaled[:, n % 2, :].rearrange("p (k s) -> p k s", k=4), ACT.Copy).then_inc(ot_hi, 1)
                elif kind == "residual" and it[1] == 2:
                    residual_squares(0)
                elif kind == "ffnturn":
                    ffn_turn(it[1])

            for i in range(FFN0):
                for it in PLAN.get(i, []):
                    if it[0] == "oturn":
                        act.wait_ge(o_ready, it[1] * 2 + it[2] + 1)
                    item(it)
                if i % 2 and (i - 1 + RING - LAG_HI) // 2 >= EARLY_HI:
                    split_pair((i - 1 + RING - LAG_HI) // 2)

            def gated(c, done, first, halves=range(SH)):
                if first:
                    act.wait_ge(rstd_ready, rstd_count["ffn"])
                for s in halves:
                    act.wait_ge(*((blk_done, done) if s else (gu_half, c + 1)))
                    if not first:
                        act.wait_ge(hid_ready, c * 2 + (s - 1))
                    act.activation(silu[:, s, :], bank[4 + s][:, 0:FC], ACT.Silu,
                                   scale=rstd[:, 6 + s:7 + s]).then_inc(silu_done, 1)

            def hidden_hi(c, dst=hidden[0]):
                act.wait_ge(ht_pe, c + 1)
                act.activation(dst, bank[6][:], ACT.Copy).then_inc(ht_hi, 1)

            split_pair(37)
            item(("ffnturn", 2))
            item(("ffnturn", 3))
            residual_squares(1)
            act.activation(warm_out[:, 1:2], warm[:, 0:1], ACT.Silu)
            split_pair(38)
            split_pair(39)
            gated(0, STEP1, True, [0])
            split_pair(40)
            gated(0, STEP1, True, [1])
            act.dma_start(gain_out[:], final_norm.partition_broadcast(P)).then_inc(in_gout, 16)

            def step(c, pairs):
                def split(m):
                    if m < pairs:
                        q = (HI0 + m) // 2
                        split_hi(2 * (HI0 + m) % RING, q % NQ, c * 16 + 16 * (q // NQ),
                                 c * STEP_BLOCKS + (2 * (HI0 + m) - 10 - STEP_BLOCKS))
                split(0)
                hidden_hi(c - 1)
                for m in range(1, 4):
                    split(m)
                gated(c, c * STEP_BLOCKS + (STEP1 - STEP_BLOCKS + GU_BLOCKS), False)
                split(4)
                split(5)

            with act.Fori(1, NCH - 1) as c:
                step(c, 6)
            step(NCH - 1, PAIRS - HI0 - (NCH - 2) * STEP_BLOCKS // 2)
            hidden_hi(NCH - 1, hidden_last[0])

            def finish(s, n):
                act.wait_ge(rstd_ready, rstd_count["final"] + s)
                act.wait_ge(gained, 2 * s + n + 1)
                act.activation(normed[:, s, n, :], normed[:, s, n, :], ACT.Copy,
                               scale=rstd[:, 8 + s:9 + s]).then_inc(fin_ready, 1)

            for s in range(SH):
                for n in range(2):
                    act.wait_ge(res_done, 8 + 2 * s + n + 1)
                    sum_squares(xs[:, s, n * NB:(n + 1) * NB], NB, (ssq2 if n else ssq)[:, 8 + s:9 + s],
                                MEAN_SCALE)
                    if s == 1:
                        finish(0, n)
            finish(1, 1)

        @block.vector
        def _(dve):
            dve.memset(warm[:], 0.0).then_inc(warm_ready, 1)

            def split_lo(slot, ready):
                dve.wait_ge(hi_ready, ready)
                dve.tensor_tensor(w_lo[:, slot:slot + 2, :], raw[:, slot:slot + 2, :],
                                  w_hi[:, slot:slot + 2, :].bitcast(f32), ALU.subtract).then_inc(lo_ready, 1)

            def split_pair(p):
                split_lo(2 * p % RING, p + 1)

            def ffn_turn(n):
                dve.wait_ge(xt_hi, KT + 2 * n + 2)
                for a in range(2):
                    k = 2 * n + a
                    dve.scalar_tensor_tensor(x_lo[:, k, :], bank[4 + n][:, a * SEQ:(a + 1) * SEQ],
                                             gain[:, G_FFN + k:G_FFN + k + 1], x_hi[:, k, :].bitcast(f32),
                                             ALU.mult, ALU.subtract).then_inc(xt_lo, 1)

            for k in range(KT):
                dve.wait_ge(xt_hi, k + 1)
                dve.scalar_tensor_tensor(x_lo[:, k, :], xT[:, k, :], gain[:, G_ATTN + k:G_ATTN + k + 1],
                                         x_hi[:, k, :].bitcast(f32), ALU.mult, ALU.subtract).then_inc(xt_lo, 1)
                dve.wait_ge(*((hi_ready, k // 2 + 1) if k % 2 else (hi_single, k // 2 + 1)))
                dve.tensor_tensor(w_lo[:, k, :], raw[:, k, :], w_hi[:, k, :].bitcast(f32),
                                  ALU.subtract).then_inc(lo_ready if k % 2 else lo_single, 1)

            def rotate(g, w, s):
                n = g * 4 + w * 2 + s
                j = 3 * g + w
                src = bank[2 * (j % 2) + s][:].rearrange("p (h d) -> p h d", h=GH)
                swapped = bank[2 * (j % 2) + s][:].rearrange("p (h a d) -> p h a d", h=GH, a=2)[:, :, ::-1, :]
                cos, sin = rotary[:, s, 0:HEAD_DIM], rotary[:, s, HEAD_DIM:2 * HEAD_DIM]
                dve.wait_ge(blk_done, j * KT + KT)
                if g == w == 0:
                    dve.wait_ge(rotary_ready, s + 1)
                if n:
                    dve.wait_ge(rotated, n)
                dve.tensor_tensor(rope_a[:].rearrange("p (h d) -> p h d", h=GH), src,
                                  cos.unsqueeze(1).to_broadcast([P, GH, HEAD_DIM]), ALU.mult).then_inc(rope_mul, 1)
                dve.tensor_tensor(rope_b[:].rearrange("p (h a d) -> p h a d", h=GH, a=2), swapped,
                                  sin.rearrange("p (a d) -> p a d", a=2).unsqueeze(1)
                                  .to_broadcast([P, GH, 2, HEAD_DIM // 2]), ALU.mult).then_inc(rope_mul, 1)
                dve.wait_ge(rope_mul, 2 * n + 2)
                if g:
                    dve.wait_ge(turned, 2 * w + s + 1)
                dve.tensor_tensor(rot[:, w, s, :], rope_a[:], rope_b[:], ALU.add).then_inc(rotated, 1)

            def item(it):
                kind = it[0]
                if kind == "rope":
                    if it == ("rope", 0, 0):
                        dve.wait_ge(in_tab, 16)
                        dve.wait_ge(rstd_ready, rstd_count["attn"])
                        for s in range(SH):
                            c = C_ROPE + s * 2 * HEAD_DIM
                            dve.tensor_scalar(rotary[:, s, :], tab[:, c:c + 2 * HEAD_DIM], rstd[:, s:s + 1], None,
                                              ALU.mult).then_inc(rotary_ready, 1)
                    rotate(it[1] // 3, it[1] % 3, it[2])
                elif kind == "turn":
                    _, g, qk_i, s = it
                    at = (slice(None), qk_i, slice(None), slice(s * P, (s + 1) * P))
                    dve.wait_ge(qk_hi, g * 4 + qk_i * 2 + s + 1)
                    if s == 0:
                        dve.tensor_tensor(qkT_lo[at], qkT_first[:, qk_i, :, :], qkT_hi[at].bitcast(f32),
                                          ALU.subtract).then_inc(qk_lo, 1)
                    else:
                        dve.scalar_tensor_tensor(qkT_lo[at], bank[TURN_BANK[qk_i][s]][:].rearrange(
                            "p (h s) -> p h s", h=HPAIRS), 1.0 if qk_i else HEAD_DIM ** -0.5,
                            qkT_hi[at].bitcast(f32), ALU.mult, ALU.subtract).then_inc(qk_lo, 1)
                elif kind == "score":
                    _, g, u = it
                    if it == ("score", 0, 0):
                        dve.wait_ge(in_mask, 16)
                    dve.wait_ge(scored, g * 3 + u + 1)
                    for t in (2 * u, 2 * u + 1):
                        half, heads, keys = attention_tile(t)
                        T = g * SC_TILES + t
                        if T >= 4:
                            old = (("probs", 0, T - 4) if T - 4 < SC_TILES else ("probs", 1, T - 4 - SC_TILES))
                            dve.wait_ge(b6_full, BANK6[old] + 1)
                        m0 = C_MASK + g * MASK_W + half * P
                        for i, head in enumerate(heads):
                            ins = dve.tensor_tensor_reduce(
                                out=probs[:, T % 4, i * keys:(i + 1) * keys],
                                in0=bank[4 + t % 2][:, i * keys:(i + 1) * keys], in1=tab[:, m0:m0 + keys],
                                scale=-1.0, scalar=3.0e38, op0=ALU.add, op1=ALU.min,
                                accum_out=neg_max[:, g, half, head:head + 1])
                        ins.then_inc(max_ready, 1)
                elif kind == "probs":
                    T = it[1] * SC_TILES + it[2]
                    dve.wait_ge(b6_full, BANK6[it] + 1)
                    if T >= 2:
                        dve.wait_ge(valued, T - 1)
                    dve.tensor_copy(probsT[:, T % 2, :], bank[6][:]).then_inc(b6_free, 1)
                elif kind == "values" and it[2] in (1, SC_TILES - 1):
                    _, g, t = it
                    half = attention_tile(t)[0]
                    n = g * 2 + half
                    dve.wait_ge(exp_done, g * SC_TILES + t + 1)
                    dve.reciprocal(rsums[:, g, half, :], sums[:, g, half, :]).then_inc(rsum_ready, 1)
                    dve.wait_ge(valued, g * SC_TILES + t + 1)
                    dve.wait_ge(rsum_ready, n + 1)
                    dve.tensor_tensor(o_sb[:, g, half, :].rearrange("p (h d) -> p h d", h=GH),
                                      bank[7][:].rearrange("p (h d) -> p h d", h=GH),
                                      rsums[:, g, half, :].unsqueeze(2).to_broadcast([P, GH, HEAD_DIM]),
                                      ALU.mult).then_inc(o_ready, 1)
                elif kind == "oturn":
                    _, g, s = it
                    n = g * 2 + s
                    col = G_MIX + 4 * g
                    dve.wait_ge(b6_full, BANK6[it] + 1)
                    if n >= 2:
                        dve.wait_ge(ot_lo, n - 1)
                    dve.tensor_tensor(scaled[:, n % 2, :].rearrange("p (k s) -> p k s", k=4),
                                      bank[6][:].rearrange("p (k s) -> p k s", k=4),
                                      gain[:, col:col + 4].unsqueeze(2).to_broadcast([P, 4, P]),
                                      ALU.mult).then_inc(b6_free, 1)
                    dve.wait_ge(ot_hi, n + 1)
                    dve.tensor_tensor(o_lo[:, g * 4:g * 4 + 4, s * P:(s + 1) * P],
                                      scaled[:, n % 2, :].rearrange("p (k s) -> p k s", k=4),
                                      o_hi[:, g * 4:g * 4 + 4, s * P:(s + 1) * P].bitcast(f32),
                                      ALU.subtract).then_inc(ot_lo, 1)
                elif kind == "residual":
                    g, n = it[1] // 2, it[1] % 2
                    dve.wait_ge(blk_done, QKV_BLOCKS + 8 * g + 4 * n + 4)
                    for s in range(SH):
                        dve.wait_ge(rstd_ready, rstd_count[f"o{g}{s}"])
                        if g:
                            dve.wait_ge(res_done, 2 * n + s + 1)
                        cols = xs[:, s, n * NB:(n + 1) * NB]
                        dve.scalar_tensor_tensor(cols, bank[2 * n + s][:], rstd[:, 2 + 2 * g + s:3 + 2 * g + s], cols,
                                                 ALU.mult, ALU.add).then_inc(res_done, 1)
                elif kind == "ffnturn":
                    ffn_turn(it[1])

            for i in range(FFN0):
                for it in PLAN.get(i, []):
                    item(it)
                if i % 2 and (i - 1 + RING - LAG_LO) // 2 >= SINGLES // 2:
                    split_pair((i - 1 + RING - LAG_LO) // 2)

            def multiply(c, halves=range(SH)):
                for s in halves:
                    dve.wait_ge(silu_done, c * 2 + (s + 1))
                    dve.scalar_tensor_tensor(hid[:, s, :], bank[4 + s][:, FC:2 * FC], rstd[:, 6 + s:7 + s],
                                             silu[:, s, :], ALU.mult, ALU.mult).then_inc(hid_ready, 1)

            def hidden_lo(c, parts=hidden):
                dve.wait_ge(ht_hi, c + 1)
                dve.tensor_tensor(parts[1], bank[6][:], parts[0].bitcast(f32), ALU.subtract).then_inc(ht_lo, 1)

            split_pair(36)
            item(("ffnturn", 2))
            item(("ffnturn", 3))
            split_pair(37)
            split_pair(38)
            multiply(0, [0])
            split_pair(39)
            multiply(0, [1])

            def step(c, pairs):
                def split(m):
                    if m < pairs:
                        split_lo(2 * (LO0 + m) % RING, c * (STEP_BLOCKS // 2) + (LO0 + m + 1 - STEP_BLOCKS // 2))
                split(0)
                hidden_lo(c - 1)
                for m in range(1, 4):
                    split(m)
                multiply(c)
                split(4)
                split(5)

            with dve.Fori(1, NCH - 1) as c:
                step(c, 6)
            step(NCH - 1, PAIRS - LO0 - (NCH - 2) * STEP_BLOCKS // 2)
            hidden_lo(NCH - 1, hidden_last)
            def with_gain(s, n):
                dve.wait_ge(res_done, 8 + 2 * s + n + 1)
                dve.tensor_tensor(normed[:, s, n, :], xs[:, s, n * NB:(n + 1) * NB],
                                  gain_out[:, n * NB:(n + 1) * NB], ALU.mult).then_inc(gained, 1)

            dve.wait_ge(in_gout, 16)
            for s in range(SH):
                for n in range(2):
                    cols = xs[:, s, n * NB:(n + 1) * NB]
                    dve.wait_ge(blk_done, BLOCKS - 4 + 2 * s + n + 1)
                    dve.tensor_tensor(cols, bank[2 * n + s][:], cols, ALU.add).then_inc(res_done, 1)
                    if s == 1:
                        with_gain(0, n)
            for n in range(2):
                with_gain(1, n)
            dve.wait_ge(rstd_ready, rstd_count["final"] + 1)
            dve.wait_ge(gained, 3)
            dve.tensor_scalar(normed[:, 1, 0, :], normed[:, 1, 0, :], rstd[:, 9:10], None, ALU.mult).then_inc(fin_dve, 1)

        @block.gpsimd
        def _(pool):
            pool.memset(neg_half[:], -0.5).then_inc(consts_ready, 1)
            pool.wait_ge(consts_ready, 1)
            made = [0]

            def link(ins):
                made[0] += 1
                ins.then_inc(msq_step, 1)
                pool.wait_ge(msq_step, made[0])

            def inverse_rms(cols, width, squares):
                pool.wait_ge(sq_done, squares)
                c = slice(*cols)
                link(pool.tensor_scalar(msq[:, c], ssq[:, c], 1.0 / width, EPS, ALU.mult, ALU.add))
                pool.tensor_tensor(rstd[:, c], msq[:, c], neg_half[:, c], ALU.pow).then_inc(rstd_ready, 1)

            def inverse_rms_of_parts(cols, first, second):
                c = slice(*cols)
                pool.wait_ge(sq_done, first)
                link(pool.tensor_scalar(msq[:, c], ssq[:, c], 1.0, EPS, ALU.mult, ALU.add))
                pool.wait_ge(sq_done, second)
                link(pool.tensor_tensor(msq[:, c], msq[:, c], ssq2[:, c], ALU.add))
                pool.tensor_tensor(rstd[:, c], msq[:, c], neg_half[:, c], ALU.pow).then_inc(rstd_ready, 1)

            inverse_rms((0, 2), D_MODEL, 2)
            for n in range(4):
                inverse_rms((2 + n, 3 + n), GW, 3 + n)
            inverse_rms_of_parts((6, 8), 8, 10)
            for s in range(SH):
                inverse_rms_of_parts((8 + s, 9 + s), 11 + 2 * s, 12 + 2 * s)


def kernel(**inputs):
    import numpy as np
    import concourse.bacc as bacc
    from concourse.bass_utils import run_bass_kernel_spmd

    table = np.zeros((P, C_END), np.float32)
    table[:, C_ID:C_ID + P] = np.eye(P)
    inv_freq = np.float32(10000.0) ** (-np.arange(0, HEAD_DIM, 2, dtype=np.float32) / np.float32(HEAD_DIM))
    ang = np.arange(SEQ, dtype=np.float32)[:, None] * inv_freq[None, :].astype(np.float32)
    half = HEAD_DIM // 2
    for s in range(SH):
        a = ang[s * P:(s + 1) * P]
        c0 = C_ROPE + s * 2 * HEAD_DIM
        s0 = c0 + HEAD_DIM
        table[:, c0:c0 + half] = table[:, c0 + half:c0 + HEAD_DIM] = np.cos(a)
        table[:, s0 + half:s0 + HEAD_DIM] = np.sin(a)
        table[:, s0:s0 + half] = -np.sin(a)
    t, k = np.arange(SEQ)[:, None], np.arange(SEQ)[None, :]
    rel = t - k
    seen = [(rel >= 0).astype(int), sum(((rel >= 0) & (rel <= w) & (rel % d == 0)).astype(int)
                                        for w, d in ((128, 1), (512, 4), (2048, 16)))]
    for g in range(2):
        m = np.where(seen[g] > 0, np.log(np.maximum(seen[g], 1)), -1e30).astype(np.float32)
        m0 = C_MASK + g * MASK_W
        table[:, m0:m0 + P] = m[:P, :P]
        table[:, m0 + P:m0 + MASK_W] = m[P:, :]

    nc = bacc.Bacc("TRN2", target_bir_lowering=False, num_devices=1)
    get = {n: np.ascontiguousarray(a) for n, a in inputs.items()}

    def quads(w):
        return [np.concatenate(list(w[i:i + QUAD]), axis=1) for i in range(0, len(w), QUAD)]

    loads = []
    for j in range(6):
        c0 = (j % 3) * D_MODEL + (j // 3) * GW
        loads += quads(get["w_in"][:, c0:c0 + NB].reshape(KT, P, NB))
    for g in range(2):
        for n in range(2):
            loads += quads(get["w_out"][g * GW:(g + 1) * GW, n * NB:(n + 1) * NB].reshape(4, P, NB))

    def gate_up(c):
        cols = slice(c * FC, (c + 1) * FC)
        return quads(np.concatenate([get["w_gate"][:, cols], get["w_up"][:, cols]], axis=1).reshape(KT, P, NB))

    def down(c):
        w = get["w_down"][c * FC:(c + 1) * FC].reshape(FT, P, 2, NB).transpose(0, 2, 1, 3)
        return quads(w.reshape(FT * 2, P, NB))

    loads += gate_up(0)
    for c in range(1, NCH):
        loads += gate_up(c) + down(c - 1)
    loads += down(NCH - 1)
    x = get["x"]
    x_turned = x[0].T.reshape(KT, P, SEQ).transpose(1, 0, 2)
    gains = np.concatenate([get[n].reshape(-1, P) for n in ("attn_norm", "moba_out_norm", "dil_out_norm",
                                                            "ffn_norm")]).T
    arrays, args = {}, []
    for name, a in (("x", x), ("x_turned", x_turned), ("weights", np.stack(loads)), ("gains", gains),
                    ("final_norm", get["final_norm"]), ("table", table)):
        a = arrays[f"in_{name}"] = np.ascontiguousarray(a)
        args.append(nc.dram_tensor(f"in_{name}", a.shape, mybir.dt.from_np(a.dtype), kind="ExternalInput").ap())
    args.append(nc.dram_tensor("out_0", (1, SEQ, D_MODEL), mybir.dt.float32, kind="ExternalOutput").ap())
    build(nc, *args)
    r = run_bass_kernel_spmd(nc, [arrays], core_ids=[0])
    return r.results[0]["out_0"]
```
